# Optimizing a Trainium2 kernel written in Bass

```python
import jax, jax.numpy as jnp
from jax import lax
import numpy as np

D_MODEL = 1024
BATCH = 1
SEQ = 256
DEPTH = 1

MEM_LEN = 256
EPS = 1e-6

HG_HEADS = 4
HG_FDIM = 128
HG_IDIM = 128
HG_WIDTH = HG_HEADS * HG_IDIM
GLA_HEADS = 4
GLA_KDIM = 64
GLA_VDIM = 128
GLA_WIDTH = GLA_HEADS * GLA_VDIM
GLA_GATE_RANK = 16
GLA_GATE_NORMALIZER = 16.0
MIX_WIDTH = HG_WIDTH + GLA_WIDTH
CHUNK = 64
IN_SPLITS = (HG_HEADS * HG_FDIM,
             HG_HEADS * HG_FDIM,
             HG_WIDTH,
             HG_WIDTH,
             GLA_HEADS * GLA_KDIM,
             GLA_HEADS * GLA_KDIM,
             GLA_WIDTH,
             GLA_WIDTH,
             GLA_GATE_RANK)
IN_WIDTH = sum(IN_SPLITS)

XA_HEADS = 4
XA_HDIM = D_MODEL // XA_HEADS

N_EXPERTS = 32
TOP_K = 4
D_EXPERT = D_MODEL
SWIGLU_LIMIT = 7.0
SWIGLU_ALPHA = 1.702
MOE_BLOCK = 256

kernel_name = "hybrid_hgrn2_gla_xattn_moe"

def rmsnorm(x, w):
    xf = x.astype(jnp.float32)
    y = xf * lax.rsqrt(jnp.mean(xf * xf, axis=-1, keepdims=True) + EPS)
    return (y * w.astype(jnp.float32)).astype(x.dtype)

def split_heads(a, n):
    b, t, _ = a.shape
    return a.reshape(b, t, n, -1).transpose(0, 2, 1, 3)

def chunked_gated_recurrence(q, k, v, g, scale):
    B, H, T, K = q.shape
    V = v.shape[-1]
    n = T // CHUNK

    def to_chunks(a):
        return a.reshape(B, H, n, CHUNK, a.shape[-1]).transpose(2, 0, 1, 3, 4)

    qc, kc, vc = to_chunks(q * scale), to_chunks(k), to_chunks(v)
    gc = to_chunks(g.astype(jnp.float32))
    causal = jnp.tril(jnp.ones((CHUNK, CHUNK), dtype=bool))[:, :, None]

    def step(S, inp):
        qb, kb, vb, gb = inp
        b = jnp.cumsum(gb, axis=2)
        diff = b[:, :, :, None, :] - b[:, :, None, :, :]
        decay = jnp.exp(jnp.where(causal, diff, -jnp.inf))
        scores = jnp.einsum('bhik,bhjk,bhijk->bhij', qb, kb, decay)
        o = (jnp.einsum('bhij,bhjv->bhiv', scores, vb)
             + jnp.einsum('bhik,bhkv->bhiv', qb * jnp.exp(b), S))
        b_last = b[:, :, -1:, :]
        S_new = (jnp.exp(b_last[:, :, 0, :])[..., None] * S
                 + jnp.einsum('bhjk,bhjv->bhkv', kb * jnp.exp(b_last - b), vb))
        return S_new, o

    S0 = jnp.zeros((B, H, K, V), jnp.float32)
    _, o = lax.scan(step, S0, (qc, kc, vc, gc))
    return o.transpose(1, 2, 0, 3, 4).reshape(B, H, T, V).astype(v.dtype)

def gated_head_norm(o, gate, w):
    b, h, t, vd = o.shape
    o = rmsnorm(o.transpose(0, 2, 1, 3), w)
    return (o * jax.nn.silu(gate.reshape(b, t, h, vd))).reshape(b, t, h * vd)

def token_mix(h, w_in, lb, hg_onorm_w, gla_w_gk2, gla_b_gk, gla_onorm_w, w_out):
    f32 = jnp.float32
    proj = h @ w_in
    idx = np.cumsum(IN_SPLITS)[:-1].tolist()
    (hq, hf, hi, hgate, gq, gk_, gv, ggate, glr) = jnp.split(proj, idx, axis=-1)

    f = lb + (1.0 - lb) * jax.nn.sigmoid(hf.astype(f32))
    hk = (1.0 - f).astype(h.dtype)
    hlogf = jnp.log(f)
    o_hg = chunked_gated_recurrence(split_heads(jax.nn.silu(hq), HG_HEADS),
                                    split_heads(hk, HG_HEADS),
                                    split_heads(hi, HG_HEADS),
                                    split_heads(hlogf, HG_HEADS), 1.0)
    y_hg = gated_head_norm(o_hg, hgate, hg_onorm_w)

    gdecay = jax.nn.log_sigmoid((glr @ gla_w_gk2 + gla_b_gk).astype(f32)) / GLA_GATE_NORMALIZER
    o_gla = chunked_gated_recurrence(split_heads(gq, GLA_HEADS),
                                     split_heads(gk_, GLA_HEADS),
                                     split_heads(gv, GLA_HEADS),
                                     split_heads(gdecay, GLA_HEADS), GLA_KDIM ** -0.5)
    y_gla = gated_head_norm(o_gla, ggate, gla_onorm_w)

    return jnp.concatenate([y_hg, y_gla], axis=-1) @ w_out

def cross_attend(h, m, w_xq, w_xkv, w_xo):
    b, t, d = h.shape
    q = (h @ w_xq).reshape(b, t, XA_HEADS, XA_HDIM)
    k, v = jnp.split(m @ w_xkv, 2, axis=-1)
    k = k.reshape(b, -1, XA_HEADS, XA_HDIM)
    v = v.reshape(b, -1, XA_HEADS, XA_HDIM)
    s = jnp.einsum('bthd,bmhd->bhtm', q, k).astype(jnp.float32) * (XA_HDIM ** -0.5)
    p = jax.nn.softmax(s, axis=-1).astype(v.dtype)
    o = jnp.einsum('bhtm,bmhd->bthd', p, v).reshape(b, t, d)
    return o @ w_xo

def moe(h, w_router, b_router, w_gate_up, b_gate_up, w_down, b_down):
    b, t, d = h.shape
    n_tok = b * t
    h2 = h.reshape(n_tok, d)
    logits = (h2 @ w_router + b_router).astype(jnp.float32)
    top_v, top_i = lax.top_k(logits, TOP_K)
    gates = jax.nn.softmax(top_v, axis=-1).astype(h.dtype)

    n_assign = n_tok * TOP_K
    flat_e = top_i.reshape(-1).astype(jnp.int32)
    flat_tok = jnp.arange(n_assign, dtype=jnp.int32) // TOP_K
    flat_g = gates.reshape(-1)
    order = jnp.argsort(flat_e, stable=True)
    se, stok, sg = flat_e[order], flat_tok[order], flat_g[order]

    counts = jnp.bincount(flat_e, length=N_EXPERTS).astype(jnp.int32)
    starts = jnp.cumsum(counts) - counts
    padded = (counts + MOE_BLOCK - 1) // MOE_BLOCK * MOE_BLOCK
    pends = jnp.cumsum(padded)
    pstarts = pends - padded
    dest = pstarts[se] + (jnp.arange(n_assign, dtype=jnp.int32) - starts[se])

    n_rows = -(-n_assign // MOE_BLOCK) * MOE_BLOCK + N_EXPERTS * MOE_BLOCK
    n_blocks = n_rows // MOE_BLOCK
    row_tok = jnp.zeros((n_rows,), jnp.int32).at[dest].set(stok)
    row_g = jnp.zeros((n_rows,), h.dtype).at[dest].set(sg)
    block_starts = jnp.arange(n_blocks, dtype=jnp.int32) * MOE_BLOCK
    block_e = jnp.clip(jnp.searchsorted(pends, block_starts, side='right'), 0, N_EXPERTS - 1)

    def expert_block(args):
        xb, e = args
        gu = xb @ w_gate_up[e] + b_gate_up[e]
        gate, up = gu[:, :D_EXPERT], gu[:, D_EXPERT:]
        gate = jnp.minimum(gate, SWIGLU_LIMIT)
        up = jnp.clip(up, -SWIGLU_LIMIT, SWIGLU_LIMIT)
        act = (up + 1.0) * gate * jax.nn.sigmoid(SWIGLU_ALPHA * gate)
        return act @ w_down[e] + b_down[e]

    xb = h2[row_tok].reshape(n_blocks, MOE_BLOCK, d)
    yb = lax.map(expert_block, (xb, block_e)).reshape(n_rows, d)
    y = jnp.zeros_like(h2).at[row_tok].add(yb * row_g[:, None])
    return y.reshape(b, t, d)

def setup_inputs(seed: int = 0) -> dict:
    key = jax.random.key(seed)
    ks = jax.random.split(key, 24)
    f32 = jnp.float32
    nrm = lambda k, shape, scale: jax.random.normal(k, shape, f32) * scale
    gain = lambda k, shape: 1.0 + 0.05 * jax.random.normal(k, shape, f32)
    L, D, E, F = DEPTH, D_MODEL, N_EXPERTS, D_EXPERT
    return {
        "x": nrm(ks[0], (BATCH, SEQ, D), 1.0),
        "mem": nrm(ks[1], (BATCH, MEM_LEN, D), 1.0),
        "norm_mix_w": gain(ks[2], (L, D)),
        "w_in": nrm(ks[3], (L, D, IN_WIDTH), D ** -0.5),
        "hg_lb_logits": nrm(ks[4], (L + 1, HG_HEADS * HG_FDIM), 0.1),
        "hg_onorm_w": gain(ks[5], (L, HG_IDIM)),
        "gla_w_gk2": nrm(ks[6], (L, GLA_GATE_RANK, GLA_HEADS * GLA_KDIM), GLA_GATE_RANK ** -0.5),
        "gla_b_gk": nrm(ks[7], (L, GLA_HEADS * GLA_KDIM), 0.1),
        "gla_onorm_w": gain(ks[8], (L, GLA_VDIM)),
        "w_out": nrm(ks[9], (L, MIX_WIDTH, D), MIX_WIDTH ** -0.5),
        "norm_xa_w": gain(ks[10], (L, D)),
        "norm_mem_w": gain(ks[11], (L, D)),
        "w_xq": nrm(ks[12], (L, D, D), D ** -0.5),
        "w_xkv": nrm(ks[13], (L, D, 2 * D), D ** -0.5),
        "w_xo": nrm(ks[14], (L, D, D), D ** -0.5),
        "norm_moe_w": gain(ks[15], (L, D)),
        "w_router": nrm(ks[16], (L, D, E), D ** -0.5),
        "b_router": nrm(ks[17], (L, E), 0.01),
        "w_gate_up": nrm(ks[18], (L, E, D, 2 * F), D ** -0.5),
        "b_gate_up": nrm(ks[19], (L, E, 2 * F), 0.01),
        "w_down": nrm(ks[20], (L, E, F, D), F ** -0.5),
        "b_down": nrm(ks[21], (L, E, D), 0.01),
        "norm_final_w": gain(ks[22], (D,)),
    }

def reference(x, mem, norm_mix_w, w_in, hg_lb_logits, hg_onorm_w, gla_w_gk2, gla_b_gk,
              gla_onorm_w, w_out, norm_xa_w, norm_mem_w, w_xq, w_xkv, w_xo, norm_moe_w,
              w_router, b_router, w_gate_up, b_gate_up, w_down, b_down, norm_final_w):
    lbs = jnp.cumsum(jax.nn.softmax(hg_lb_logits.astype(jnp.float32), axis=0), axis=0)
    for l in range(DEPTH):
        h = rmsnorm(x, norm_mix_w[l])
        x = x + token_mix(h, w_in[l], lbs[l], hg_onorm_w[l], gla_w_gk2[l], gla_b_gk[l],
                          gla_onorm_w[l], w_out[l])
        x = x + cross_attend(rmsnorm(x, norm_xa_w[l]), rmsnorm(mem, norm_mem_w[l]),
                             w_xq[l], w_xkv[l], w_xo[l])
        x = x + moe(rmsnorm(x, norm_moe_w[l]), w_router[l], b_router[l], w_gate_up[l],
                    b_gate_up[l], w_down[l], b_down[l])
    return rmsnorm(x, norm_final_w)


_drawn_inputs = setup_inputs


def setup_inputs(seed=0):
    import zlib

    import numpy as np

    out = dict(_drawn_inputs(seed))
    spreads = {}
    factors = {'hg_lb_logits': 3.645,
     'norm_xa_w': 8.0,
     'b_gate_up': 8.0,
     'b_down': 8.0,
     'b_router': 3.085}
    for name, (base, spread) in spreads.items():
        noise = np.random.default_rng([zlib.crc32(name.encode()), seed]).standard_normal(out[name].shape)
        drawn = base * np.exp(spread * noise) if base else spread * noise
        out[name] = __import__('jax').numpy.asarray(drawn.astype(out[name].dtype))
    for name, factor in factors.items():
        out[name] = (out[name] * factor).astype(out[name].dtype)
    return out
```

```python
from contextlib import ExitStack

import numpy as np

import concourse.bass as bass
from concourse import mybir

F32 = mybir.dt.float32
I32 = mybir.dt.int32
U32 = mybir.dt.uint32
ALU = mybir.AluOpType
ACT = mybir.ActivationFunctionType
AX = mybir.AxisListType

P = 128
D = 1024
T = 256
NT = T // P
KT = D // P
EPS = 1e-6
CHUNK = 64
VD = 128
HEADS = 4
QT = 6
GKD = 64
RANK = 16
GATE_NORM = 16.0
C_HQ, C_HF, C_HI, C_HG, C_GQ, C_GV, C_GG, C_GLR = 0, 512, 1024, 1536, 2048, 2560, 3072, 3584
XH = 4
E = 32
TOPK = 4
LIMIT = 7.0
ALPHA = 1.702
ROWS = 64
MAXB = T // ROWS
CHUNKS = 12
GU_CHUNKS = KT
PW = 512
SLOTS = 6


PANELS = [("w_in", C_HF, "hf1"), ("w_in", C_HQ, "hq1"), ("w_in", C_GQ, "gk"), ("w_in", C_HI, "hi1"),
          ("w_in", C_GV, "gv1"), ("w_in", C_HG, "hg1"), ("w_in", C_GG, "gg1"), ("w_xkv", 0, "xk1"),
          ("w_xkv", PW, "xk3"), ("w_xkv", 2 * PW, "xv01"), ("w_out", 0, "out01"), ("w_out", PW, "out11"),
          ("w_xkv", 3 * PW, "xv11"), ("w_xq", 0, "xq1"), ("w_xq", PW, "xq3"), ("w_xo", 0, "xo01"), ("w_xo", PW, "xo11")]
LEVELS = [1, 2, 4, 8, 16, 32, 64, 128]


def four(name):
    return [f"{name}{t}{h}" for t in range(2) for h in range(2)]


def level_jobs(s):
    return [f"lv{s}_h{t}" for t in range(NT if s < P else 1)] + [f"lv{s}_g{half}" for half in range(2)]


JOBS = (four("xT") + ["hf0", "hf1", "glr", "z"] + four("mT") + ["hq0", "hq1", "fT0", "fT1", "b0", "b1", "b2", "gq", "gk"]
        + ["hi0", "hi1"] + level_jobs(1) + ["gv0", "gv1"] + level_jobs(2) + ["hg0", "hg1"] + level_jobs(4)
        + ["gg0", "gg1"] + level_jobs(8) + ["xk0", "xk1"] + level_jobs(16) + ["xk2", "xk3"] + level_jobs(32)
        + level_jobs(64) + ["xv00", "xv01"] + level_jobs(128) + ["diag", "o0h", "o0g", "o1h", "o1g", "xv10"]
        + four("yT") + four("out") + ["xv11"] + four("aT") + ["xq0", "xq1", "xq2", "xq3"] + four("sc")
        + ["pT0", "pT1", "pT2", "pT3", "pv0", "pv1", "pv2", "pv3"] + four("xo") + ["bias"] + four("eT")
        + ["router", "rank", "count", "table", "gT"])

SEMS = """x_in w_mix_in mem_in vec_in lb_in glr_in gk_bias_in router_in moe_row_in final_row_in bias_in
 consts_ready masks_ready s_zeroed x_squared x_normed mem_squared mem_normed lb_diff lb_exp f_ready lnf_ready
 z_abs z_exp z_ln g_ready hq_exp k_ready r_diff r_exp r_ready gate_exp gate_ready y_ready x1_squared x1_normed
 neg_max p_exp p_ready x2_squared h2_ready gate_max gate_exps chosen_ready nb_ready gates_ready up_gated mean_ready root_ln root_guess
 dve_step pool_step swiglu_step sel_ready xb_psum xb_ready yb0_psum yb0_ready comb_psum
 comb_ready yb1_psum yb1_ready gate_done g_clamped sig_ready act_ready selg_ready chunk_used yT_ready
 scattered out_summed out_squared out_ready stored""".split()


def build(nc, A, out):
    ctx = ExitStack()
    with ctx:
        ctx.enter_context(nc.allow_non_contiguous_dma("small vectors are laid out by feature"))

        def sb(name, cols, dt=F32, rows=P):
            return ctx.enter_context(nc.sbuf_tensor(name, [rows, cols], dt))

        sem = {n: ctx.enter_context(nc.semaphore(n)) for n in SEMS}
        bank_full = [ctx.enter_context(nc.semaphore(f"bank_full{b}")) for b in range(8)]
        bank_taken = [ctx.enter_context(nc.semaphore(f"bank_taken{b}")) for b in range(8)]
        panel_in = [ctx.enter_context(nc.semaphore(f"panel_in{s}")) for s in range(SLOTS)]
        chunk_in = [ctx.enter_context(nc.semaphore(f"chunk_in{k}")) for k in range(CHUNKS)]
        banks = [ctx.enter_context(nc.psum_tensor(f"bank{b}", [P, 512], F32)) for b in range(8)]

        ring = sb("ring", CHUNKS * 2048)
        x_res_t = sb("x_res", NT * D)
        region1 = sb("region1", KT * T)
        region2 = sb("region2", KT * T)
        region3 = sb("region3", KT * T)
        region5 = sb("region5", NT * D)
        region6 = sb("region6", NT * D)
        region7 = sb("region7", 3 * QT * T)
        region10 = sb("region10", NT * D)
        r_t = sb("r_levels", 2 * QT * T)
        s_t = sb("s_matrices", 2 * HEADS * 3 * P)
        tmp_t = sb("tmp", 1024)
        row_t = sb("rows", 1024)
        ident = sb("ident", P)
        tri = sb("tri", P)
        strict = sb("strict", P)
        ones = sb("ones", P)
        iota = sb("iota", T)
        onorm = sb("onorm", 2 * VD)
        cols = sb("norm_cols", 3 * KT)
        stat = sb("stat", 88)
        idx8 = sb("idx8", NT * 8, U32)
        table = sb("table", 3 * E + 1, I32, rows=1)

        def fm(t, off=0):
            return t[:, off:off + KT * T].rearrange("p (k t) -> p k t", t=T)

        def tm(t, off=0, n=D):
            return t[:, off:off + NT * n].rearrange("p (t n) -> p t n", n=n)

        small = region1
        x_res = tm(x_res_t)
        hT, yT, aT, oT = fm(region1), fm(region1), fm(region1), fm(region1)
        memT, qxT, h2T = fm(region2), fm(region2), fm(region2)
        f_tok = tm(region3, 0, 512)
        zb = tm(region3, 1024, 256)
        ez = tm(region3, 1536, 256)
        xkT = fm(region3)
        b_gu_raw = region3[0:E, 0:2 * D]
        mem_raw, v_tok = tm(region5), tm(region5)
        probs = region5[:, :].rearrange("p (t h m) -> p t h m", t=NT, h=XH)
        b_down_sb = region5[0:E, 0:D]
        lb2 = region6[:, 0:1024].rearrange("p (a n) -> p a n", a=2)
        squares = region6[:, 1024:2048]
        gates = tm(region6)
        probsT = region6[:, :].rearrange("p (h m t) -> p h m t", h=XH, m=2)
        qT = region7[:, 0:1536].rearrange("p (k t) -> p k t", t=T)
        kT = region7[:, 1536:3072].rearrange("p (k t) -> p k t", t=T)
        bT = region7[:, 3072:4608].rearrange("p (k t) -> p k t", t=T)
        w_glr = region7[:, 3072:3200].rearrange("p (k n) -> p k n", n=RANK)
        gk2 = region7[0:RANK, 3200:3456]
        glrT = region7[0:RANK, 3456:3712]
        sel = region7[:, 0:128].rearrange("p (t r) -> p t r", t=NT)[:, :, 0:ROWS]
        selg = region7[:, 128:256].rearrange("p (t r) -> p t r", t=NT)[:, :, 0:ROWS]
        xbT = region7[:, 256:256 + KT * ROWS].rearrange("p (k r) -> p k r", r=ROWS)
        combT = region7[0:ROWS, 768:768 + T]
        act_t, g_t, u_t, sg_t, yT_sb = (region7[:, c:c + KT * ROWS].rearrange("p (k r) -> p k r", r=ROWS)
                                        for c in range(1024, 3584, 512))
        yb = region7[0:ROWS, 3584:3584 + D]
        w_router = region7[:, 1024:1280].rearrange("p (k n) -> p k n", n=E)
        b_router = region7[:, 1280:1280 + E]
        gT_sb = region7[0:E, 1536:1536 + T]
        xn, h2 = tm(region10), tm(region10)
        R = r_t[:, :].rearrange("p (a k t) -> p a k t", a=2, t=T)
        o_tok = r_t[:, 0:NT * D].rearrange("p (t n) -> p t n", n=D)
        S = s_t[:, :].rearrange("p (h a i) -> p h a i", h=2 * HEADS, a=3)

        def S_gla(half):
            return S[:, HEADS + half::2, :, :]

        g_tok = tm(s_t, 0, 768)
        e_f = tm(s_t, 1536, 512)
        l_z = tm(s_t, 2560, 256)
        xv0, xv1 = tm(tmp_t, 0, 512), tm(s_t, 0, 512)
        tmp = tmp_t[:, :].rearrange("p (a n) -> p a n", a=2)
        gk_bias = tmp_t[:, 0:256]
        biasT = tmp_t[:, 0:E * 16].rearrange("p (e m) -> p e m", e=E)
        masks = row_t[:, 0:(len(LEVELS) - 1) * P].rearrange("p (l i) -> p l i", i=P)
        norm_row = row_t[:, :]
        w_mix, w_xa, w_mem = (cols[:, i * KT:(i + 1) * KT] for i in range(3))
        rstd = stat[:, 0:8]
        ssq = stat[:, 8:16]
        hsq = stat[:, 16:32].rearrange("p (t h) -> p t h", t=NT)
        hrms = stat[:, 64:80].rearrange("p (t h) -> p t h", t=NT)
        newton = stat[:, 80:88]
        dots = stat[:, 32:48].rearrange("p (t h) -> p t h", t=NT)
        nmax = stat[:, 48:56].rearrange("p (t h) -> p t h", t=NT)
        psums = stat[:, 56:64].rearrange("p (t h) -> p t h", t=NT)
        logits, chosen, gate_ex, gate_tok, rank_m = (small[:, c:c + NT * E].rearrange("p (t e) -> p t e", t=NT)
                                                     for c in range(0, 320, 64))
        top8, idxf = (small[:, c:c + NT * 8].rearrange("p (t e) -> p t e", t=NT) for c in (320, 336))
        gsum, ngmax, nb_col = small[:, 352:354], small[:, 354:356], small[0:E, 356:357]
        table_f = small[0:1, 360:360 + 3 * E]

        def panel(n):
            s = n % SLOTS
            return ring[:, s * 4096:(s + 1) * 4096].rearrange("p (k n) -> p k n", n=PW)

        def chunk(k):
            return ring[:, k * 2048:(k + 1) * 2048]

        def bank_of(job):
            return banks[JOBS.index(job) % 8]

        def wait_full(eng, job):
            n = JOBS.index(job)
            eng.wait_ge(bank_full[n % 8], n // 8 + 1)

        def wait_taken(eng, job):
            n = JOBS.index(job)
            eng.wait_ge(bank_taken[n % 8], n // 8 + 1)

        def taken(ins, job):
            ins.then_inc(bank_taken[JOBS.index(job) % 8], 1)

        bank_y = [[banks[0], banks[1]], [banks[2], banks[3]]]
        bank_a, bank_g, bank_u, bank_d = banks[4], banks[5], banks[6], banks[7]
        block = ctx.enter_context(nc.Block())

        @block.sync
        def _(sp):
            for t in range(NT):
                sp.dma_start(x_res[:, t, :], A["x"][0, t * P:(t + 1) * P, :]).then_inc(sem["x_in"], 16)
            weight = {"w_in": A["w_in"], "w_xkv": A["w_xkv"], "w_out": A["w_out"], "w_xq": A["w_xq"], "w_xo": A["w_xo"]}
            for n, (name, c0, _) in enumerate(PANELS):
                if n >= SLOTS:
                    wait_full(sp, PANELS[n - SLOTS][2])
                src = weight[name][0, :, c0:c0 + PW].rearrange("(k p) n -> p k n", p=P)
                sp.dma_start(panel(n), src).then_inc(panel_in[n % SLOTS], 16)
                if n == 0:
                    sp.dma_start(mem_raw, A["mem"][0].rearrange("(t p) n -> p t n", p=P)).then_inc(sem["mem_in"], 16)

            def load_chunk(e, k):
                if k < GU_CHUNKS:
                    src = A["w_gate_up"][0, e, k * P:(k + 1) * P, :]
                    dst = chunk(k)
                else:
                    j = k - GU_CHUNKS
                    src = A["w_down"][0, e, 2 * j * P:(2 * j + 2) * P, :].rearrange("(a p) n -> p a n", p=P)
                    dst = chunk(k).rearrange("p (a n) -> p a n", a=2)
                sp.dma_start(dst, src).then_inc(chunk_in[k], 16)

            for n in range(len(PANELS) - SLOTS, len(PANELS)):
                wait_full(sp, PANELS[n][2])
                for k in (2 * (n % SLOTS), 2 * (n % SLOTS) + 1):
                    load_chunk(0, k)
            wait_taken(sp, "table")
            with sp.Fori(1, E) as e:
                used = sp.value_load(table[0:1, bass.ds(e + 2 * E, 1)], min_val=0, max_val=CHUNKS * MAXB * E)
                for k in range(CHUNKS):
                    sp.wait_ge(sem["chunk_used"], used + (k + 1))
                    load_chunk(e, k)
            for t in range(NT):
                sp.wait_ge(sem["out_ready"], t + 1)
                sp.dma_start(out[0, t * P:(t + 1) * P, :], xn[:, t, :]).then_inc(sem["stored"], 16)
            sp.wait_ge(sem["stored"], 16 * NT)

        @block.gpsimd
        def _(pool):
            def by_feature(v):
                return v.rearrange("(k p) -> p k", p=P)

            pool.dma_start(w_mix, by_feature(A["norm_mix_w"][0])).then_inc(sem["w_mix_in"], 16)
            pool.dma_start(w_glr, A["w_in"][0, :, C_GLR:C_GLR + RANK].rearrange("(k p) n -> p k n", p=P)).then_inc(sem["glr_in"], 16)
            pool.dma_start(gk2, A["gla_w_gk2"][0]).then_inc(sem["glr_in"], 16)
            pool.dma_start(lb2, A["hg_lb_logits"].rearrange("(o a) n -> o a n", o=1).broadcast_to([P, 2, 512])).then_inc(sem["lb_in"], 16)
            pool.dma_start(gk_bias, A["gla_b_gk"].broadcast_to([P, 256])).then_inc(sem["gk_bias_in"], 16)
            steps = [0]

            def link(ins):
                steps[0] += 1
                ins.then_inc(sem["pool_step"], 1)
                pool.wait_ge(sem["pool_step"], steps[0])

            link(pool.memset(ident[:, :], 0.0))
            link(pool.affine_select(out=ident[:, :], in_=ident[:, :], compare_op=ALU.not_equal, fill=1.0, base=0,
                                    pattern=[[-1, P]], channel_multiplier=1))
            link(pool.memset(ones[:, :], 1.0))
            link(pool.affine_select(out=tri[:, :], in_=ones[:, :], compare_op=ALU.is_ge, fill=0.0, base=0,
                                    pattern=[[1, P]], channel_multiplier=-1))
            link(pool.memset(tri[0:CHUNK, CHUNK:P], 0.0))
            link(pool.affine_select(out=strict[:, :], in_=ones[:, :], compare_op=ALU.is_gt, fill=0.0, base=0,
                                    pattern=[[1, P]], channel_multiplier=-1))
            pool.iota(iota[:, :], pattern=[[1, T]], base=0, channel_multiplier=0,
                      allow_small_or_imprecise_dtypes=True).then_inc(sem["consts_ready"], 1)
            pool.dma_start(w_mem, by_feature(A["norm_mem_w"][0])).then_inc(sem["vec_in"], 16)
            pool.dma_start(w_xa, by_feature(A["norm_xa_w"][0])).then_inc(sem["vec_in"], 16)
            pool.dma_start(onorm[:, 0:VD], A["hg_onorm_w"].broadcast_to([P, VD])).then_inc(sem["vec_in"], 16)
            pool.dma_start(onorm[:, VD:2 * VD], A["gla_onorm_w"].broadcast_to([P, VD])).then_inc(sem["vec_in"], 16)
            for n, s in enumerate(LEVELS[:-1]):
                m = masks[:, n, :].rearrange("p (b a r) -> p b a r", a=2, r=s)
                link(pool.memset(masks[:, n, :], 0.0))
                link(pool.memset(m[:, :, 1, :], 1.0))
                link(pool.affine_select(out=m[:, :, 1, :], in_=m[:, :, 1, :], compare_op=ALU.is_ge, fill=0.0, base=0,
                                        pattern=[[-2 * s, P // (2 * s)], [0, s]], channel_multiplier=1))
                pool.affine_select(out=m[:, :, 1, :], in_=m[:, :, 1, :], compare_op=ALU.is_gt, fill=0.0, base=s,
                                   pattern=[[2 * s, P // (2 * s)], [0, s]], channel_multiplier=-1).then_inc(sem["masks_ready"], 1)
            for job in ("b0", "b1", "b2"):
                wait_full(pool, job)
            pool.memset(s_t[:, :], 0.0).then_inc(sem["s_zeroed"], 1)
            wait_full(pool, "diag")
            pool.dma_start(w_router, A["w_router"][0].rearrange("(k p) n -> p k n", p=P)).then_inc(sem["router_in"], 16)
            pool.dma_start(b_router, A["b_router"].broadcast_to([P, E])).then_inc(sem["router_in"], 16)
            for job in level_jobs(64):
                wait_taken(pool, job)
            pool.dma_start(norm_row, A["norm_moe_w"].broadcast_to([P, D])).then_inc(sem["moe_row_in"], 16)
            wait_full(pool, "sc11")
            pool.dma_start(b_gu_raw, A["b_gate_up"][0]).then_inc(sem["bias_in"], 16)
            wait_full(pool, "pT3")
            pool.dma_start(b_down_sb, A["b_down"][0]).then_inc(sem["bias_in"], 16)
            pool.wait_ge(sem["h2_ready"], NT)
            pool.dma_start(norm_row, A["norm_final_w"].rearrange("(o n) -> o n", o=1).broadcast_to([P, D])).then_inc(sem["final_row_in"], 16)

        @block.tensor
        def _(pe):
            done = [0]

            def begin(job):
                n = done[0]
                assert JOBS[n] == job, (JOBS[n], job)
                if n >= 8:
                    wait_taken(pe, JOBS[n - 8])
                return banks[n % 8]

            def end(ins):
                ins.then_inc(bank_full[done[0] % 8], 1)
                done[0] += 1

            def arrived(first_job_weight, c0):
                n = [p[:2] for p in PANELS].index((first_job_weight, c0))
                pe.wait_ge(panel_in[n % SLOTS], 16 * (n // SLOTS + 1))
                return panel(n)

            def transposes(prefix, src):
                for t in range(NT):
                    for h in range(2):
                        bk = begin(f"{prefix}{t}{h}")
                        for i in range(4):
                            k = 4 * h + i
                            last = pe.transpose(bk[:, i * P:(i + 1) * P], src[:, t, k * P:(k + 1) * P], ident[:, :])
                        end(last)

            def by_feature(job, w, m, rhs):
                bk = begin(job)
                for i in range(2):
                    for k in range(KT):
                        last = pe.matmul(bk[:, i * T:(i + 1) * T], w[:, k, (m + i) * P:(m + i + 1) * P], rhs[:, k, :],
                                         start=(k == 0), stop=(k == KT - 1))
                end(last)

            def by_token(job, w, t, lhs):
                bk = begin(job)
                for k in range(KT):
                    last = pe.matmul(bk[:, :], lhs[:, k, t * P:(t + 1) * P], w[:, k, :], start=(k == 0), stop=(k == KT - 1))
                end(last)

            def level(n):
                pe.wait_ge(sem["r_ready"], n + 1)
                s = LEVELS[n]
                tiles = [(t, t) for t in range(NT)] if s < P else [(0, 1)]

                def scores(out_, rows, j, i):
                    return pe.matmul(out_, rows[:, j * P:(j + 1) * P], rows[:, i * P:(i + 1) * P], start=True, stop=True)

                for j, i in tiles:
                    bk = begin(f"lv{s}_h{j}")
                    for h in range(HEADS):
                        last = scores(bk[:, h * P:(h + 1) * P], R[:, n % 2, h, :], j, i)
                    end(last)
                for half in range(2):
                    bk = begin(f"lv{s}_g{half}")
                    for h in range(2):
                        rows = R[GKD * half:GKD * (half + 1), n % 2, HEADS + h, :]
                        for a, (j, i) in enumerate(tiles):
                            c = (h * len(tiles) + a) * P
                            last = scores(bk[:, c:c + P], rows, j, i)
                    end(last)

            pe.wait_ge(sem["consts_ready"], 1)
            pe.wait_ge(sem["x_normed"], NT)
            transposes("xT", xn)
            for job in four("xT"):
                wait_taken(pe, job)
            w = arrived("w_in", C_HF)
            by_token("hf0", w, 0, hT)
            by_token("hf1", w, 1, hT)
            pe.wait_ge(sem["glr_in"], 32)
            bk = begin("glr")
            for k in range(KT):
                last = pe.matmul(bk[0:RANK, 0:T], w_glr[:, k, :], hT[:, k, :], start=(k == 0), stop=(k == KT - 1))
            end(last)
            wait_taken(pe, "glr")
            bk = begin("z")
            for t in range(NT):
                last = pe.matmul(bk[:, t * 256:(t + 1) * 256], glrT[:, t * P:(t + 1) * P], gk2, start=True, stop=True)
            end(last)
            pe.wait_ge(sem["mem_normed"], NT)
            transposes("mT", xn)
            w = arrived("w_in", C_HQ)
            by_feature("hq0", w, 0, hT)
            by_feature("hq1", w, 2, hT)
            pe.wait_ge(sem["f_ready"], NT)
            for i in range(2):
                bk = begin(f"fT{i}")
                for a in range(2):
                    for t in range(NT):
                        last = pe.transpose(bk[:, a * T + t * P:a * T + (t + 1) * P],
                                            f_tok[:, t, (2 * i + a) * P:(2 * i + a + 1) * P], ident[:, :])
                end(last)
            pe.wait_ge(sem["lnf_ready"], NT)
            pe.wait_ge(sem["g_ready"], 1)
            for i in range(3):
                bk = begin(f"b{i}")
                for a in range(2):
                    for t in range(NT):
                        last = pe.matmul(bk[:, a * T + t * P:a * T + (t + 1) * P],
                                         g_tok[:, t, (2 * i + a) * P:(2 * i + a + 1) * P], tri[:, :], start=True, stop=True)
                end(last)
            w = arrived("w_in", C_GQ)
            by_feature("gq", w, 0, hT)
            by_feature("gk", w, 2, hT)
            for n, (name, c0) in enumerate((("hi", C_HI), ("gv", C_GV), ("hg", C_HG), ("gg", C_GG))):
                w = arrived("w_in", c0)
                by_token(f"{name}0", w, 0, hT)
                by_token(f"{name}1", w, 1, hT)
                level(n)
            for job in four("mT"):
                wait_taken(pe, job)
            for i in range(2):
                w = arrived("w_xkv", i * PW)
                by_feature(f"xk{2 * i}", w, 0, memT)
                by_feature(f"xk{2 * i + 1}", w, 2, memT)
                level(4 + i)
            level(6)
            w = arrived("w_xkv", 2 * PW)
            by_token("xv00", w, 0, memT)
            by_token("xv01", w, 1, memT)
            level(7)
            pe.wait_ge(sem["r_ready"], 9)
            bk = begin("diag")
            for k in range(QT):
                for t in range(NT):
                    if k < HEADS:
                        c, n, rhs = t * 2 * HEADS + k, 1, ones[:, 0:1]
                    else:
                        c, n, rhs = t * 2 * HEADS + HEADS + 2 * (k - HEADS), 2, tri[:, CHUNK - 1::CHUNK]
                    last = pe.matmul(bk[:, c:c + n], R[:, 0, k, t * P:(t + 1) * P], rhs, start=True, stop=True)
            end(last)
            for job in level_jobs(64) + level_jobs(128) + ["hi0", "hi1", "gv0", "gv1"]:
                wait_taken(pe, job)
            for t in range(NT):
                for g, group in enumerate("hg"):
                    bk = begin(f"o{t}{group}")
                    for h in range(HEADS):
                        hh = g * HEADS + h
                        parts = [(0, 0)] if t == 0 else [(2, 0), (1, 1)]
                        for a, j in parts:
                            last = pe.matmul(bk[:, h * VD:(h + 1) * VD], S[:, hh, a, :], v_tok[:, j, hh * VD:(hh + 1) * VD],
                                             start=(j == 0), stop=(j == t))
                    end(last)
            w = arrived("w_xkv", 3 * PW)
            by_token("xv10", w, 0, memT)
            for t in range(NT):
                pe.wait_ge(sem["y_ready"], t + 1)
                for h in range(2):
                    bk = begin(f"yT{t}{h}")
                    for i in range(4):
                        k = 4 * h + i
                        last = pe.transpose(bk[:, i * P:(i + 1) * P], o_tok[:, t, k * P:(k + 1) * P], ident[:, :])
                    end(last)
            for job in four("yT"):
                wait_taken(pe, job)
            for i in range(2):
                w = arrived("w_out", i * PW)
                by_token(f"out{i}0", w, 0, yT)
                by_token(f"out{i}1", w, 1, yT)
            w = arrived("w_xkv", 3 * PW)
            by_token("xv11", w, 1, memT)
            pe.wait_ge(sem["x1_normed"], NT)
            transposes("aT", xn)
            for job in four("aT"):
                wait_taken(pe, job)
            for i in range(2):
                w = arrived("w_xq", i * PW)
                by_feature(f"xq{2 * i}", w, 0, aT)
                by_feature(f"xq{2 * i + 1}", w, 2, aT)
            for job in ["xk0", "xk1", "xk2", "xk3", "xq0", "xq1", "xq2", "xq3"]:
                wait_taken(pe, job)
            for t in range(NT):
                for h in range(2):
                    bk = begin(f"sc{t}{h}")
                    for i in range(2):
                        for a in range(2):
                            k = 2 * (2 * h + i) + a
                            last = pe.matmul(bk[:, i * T:(i + 1) * T], qxT[:, k, t * P:(t + 1) * P], xkT[:, k, :],
                                             start=(a == 0), stop=(a == 1))
                    end(last)
            pe.wait_ge(sem["p_ready"], 4)
            for h in range(XH):
                bk = begin(f"pT{h}")
                for m in range(2):
                    for t in range(NT):
                        last = pe.transpose(bk[:, m * T + t * P:m * T + (t + 1) * P], probs[:, t, h, m * P:(m + 1) * P], ident[:, :])
                end(last)
            for job in ["xv00", "xv01", "xv10", "xv11"]:
                wait_taken(pe, job)
            for h in range(XH):
                wait_taken(pe, f"pT{h}")
                bk = begin(f"pv{h}")
                for a in range(2):
                    c = (2 * (h % 2) + a) * P
                    for m in range(2):
                        last = pe.matmul(bk[:, a * T:(a + 1) * T], (xv0, xv1)[h // 2][:, m, c:c + P], probsT[:, h, m, :],
                                         start=(m == 0), stop=(m == 1))
                end(last)
            for h in range(XH):
                wait_taken(pe, f"pv{h}")
            for i in range(2):
                w = arrived("w_xo", i * PW)
                by_token(f"xo{i}0", w, 0, oT)
                by_token(f"xo{i}1", w, 1, oT)
            pe.wait_ge(sem["bias_in"], 32)
            bk = begin("bias")
            for m in range(16):
                last = pe.transpose(bk[:, m * E:(m + 1) * E], b_gu_raw[:, m * P:(m + 1) * P], ident[0:E, 0:E])
            end(last)
            pe.wait_ge(sem["h2_ready"], NT)
            transposes("eT", h2)
            for job in four("eT"):
                wait_taken(pe, job)
            pe.wait_ge(sem["router_in"], 32)
            bk = begin("router")
            for t in range(NT):
                for k in range(KT):
                    last = pe.matmul(bk[:, t * E:(t + 1) * E], h2T[:, k, t * P:(t + 1) * P], w_router[:, k, :],
                                     start=(k == 0), stop=(k == KT - 1))
            end(last)
            pe.wait_ge(sem["chosen_ready"], 1)
            bk = begin("rank")
            pe.matmul(bk[:, 0:E], strict[:, :], chosen[:, 0, :], start=True, stop=True)
            pe.matmul(bk[:, E:2 * E], ones[:, :], chosen[:, 0, :], start=True, stop=False)
            end(pe.matmul(bk[:, E:2 * E], strict[:, :], chosen[:, 1, :], start=False, stop=True))
            bk = begin("count")
            pe.matmul(bk[0:E, 0:1], chosen[:, 0, :], ones[:, 0:1], start=True, stop=False)
            end(pe.matmul(bk[0:E, 0:1], chosen[:, 1, :], ones[:, 0:1], start=False, stop=True))
            wait_taken(pe, "count")
            bk = begin("table")
            pe.matmul(bk[0:1, 0:E], nb_col, ident[0:E, 0:E], start=True, stop=True)
            end(pe.matmul(bk[0:1, E:2 * E], nb_col, strict[0:E, 0:E], start=True, stop=True))
            pe.wait_ge(sem["gates_ready"], 1)
            bk = begin("gT")
            for t in range(NT):
                last = pe.transpose(bk[0:E, t * P:(t + 1) * P], gate_tok[:, t, :], ident[:, :])
            end(last)

            for job in JOBS[-8:]:
                wait_taken(pe, job)
            for t in range(NT):
                for h in range(2):
                    pe.matmul(bank_y[t][h][:, :], gT_sb[:, t * P:(t + 1) * P], b_down_sb[:, h * 512:(h + 1) * 512],
                              start=True, stop=False, skip_group_check=True)

            def transposed(out_, in_, mode=True):
                return pe.matmul(out_, in_, ident[:, :], start=True, stop=True, is_transpose=mode, skip_group_check=True)

            def rows_of_block(h, bk, mode=True):
                for i in range(4):
                    last = transposed(bk[0:ROWS, i * P:(i + 1) * P], yT_sb[:, 4 * h + i, :], mode)
                return last

            def gates_of_block(bk, mode=True):
                for t in range(NT):
                    last = transposed(bk[0:ROWS, t * P:(t + 1) * P], selg[:, t, :], mode)
                return last

            def scatter(h):
                for t in range(NT):
                    last = pe.matmul(bank_y[t][h][:, :], combT[:, t * P:(t + 1) * P], yb[:, h * 512:(h + 1) * 512],
                                     start=False, stop=False, skip_group_check=True)
                return last

            with pe.Fori(0, E) as e:
                blocks = pe.value_load(table[0:1, bass.ds(e, 1)], min_val=1, max_val=MAXB)
                first = pe.value_load(table[0:1, bass.ds(e + E, 1)], min_val=0, max_val=MAXB * E)
                in_e = pe.snap(16 * e + 16)
                with pe.Fori(0, blocks) as c:
                    w1 = pe.snap(first + c + 1)
                    pe.wait_ge(sem["sel_ready"], w1)
                    for k in range(KT):
                        if k == KT // 2:
                            pe.wait_ge(sem["yT_ready"], w1)
                        for t in range(NT):
                            last = pe.matmul(bank_a[:, k * ROWS:(k + 1) * ROWS], h2[:, t, k * P:(k + 1) * P], sel[:, t, :],
                                             start=(t == 0), stop=(t == NT - 1), skip_group_check=True)
                    last.then_inc(sem["xb_psum"], 1)
                    rows_of_block(0, bank_d).then_inc(sem["yb0_psum"], 1)
                    pe.wait_ge(sem["xb_ready"], w1)
                    for k in range(GU_CHUNKS):
                        pe.wait_ge(chunk_in[k], in_e)
                        if k == 3:
                            pe.wait_ge(sem["selg_ready"], w1)
                            pe.wait_ge(sem["yb0_ready"], w1)
                        wk = chunk(k)
                        for m in range(16):
                            bk, i = (bank_g, m) if m < 8 else (bank_u, m - 8)
                            last = pe.matmul(bk[:, i * ROWS:(i + 1) * ROWS], wk[:, m * P:(m + 1) * P], xbT[:, k, :],
                                             start=(k == 0 and i == 0), stop=(k == KT - 1), skip_group_check=True)
                            if k == KT - 1 and m == 7:
                                last.then_inc(sem["gate_done"], 1)
                        last.then_inc(sem["chunk_used"], 1)
                        if k == 3:
                            gates_of_block(bank_d).then_inc(sem["comb_psum"], 1)
                    rows_of_block(1, bank_a).then_inc(sem["yb1_psum"], 1)
                    pe.wait_ge(sem["comb_ready"], w1)
                    scatter(0)
                    pe.wait_ge(sem["yb1_ready"], w1)
                    scatter(1)
                    pe.wait_ge(sem["act_ready"], w1)
                    for j in range(CHUNKS - GU_CHUNKS):
                        pe.wait_ge(chunk_in[GU_CHUNKS + j], in_e)
                        wj = chunk(GU_CHUNKS + j)
                        for a in range(2):
                            f = 2 * j + a
                            for m in range(KT):
                                last = pe.matmul(bank_d[:, m * ROWS:(m + 1) * ROWS], wj[:, a * D + m * P:a * D + (m + 1) * P],
                                                 act_t[:, f, :], start=(f == 0 and m == 0), stop=(f == KT - 1), skip_group_check=True)
                        last.then_inc(sem["chunk_used"], 1)
            total = pe.value_load(table[0:1, 3 * E:3 * E + 1], min_val=E, max_val=MAXB * E)
            total1 = pe.snap(total + 1)
            pe.wait_ge(sem["yT_ready"], total1)
            rows_of_block(0, bank_a, False)
            rows_of_block(1, bank_g, False).then_inc(sem["yb1_psum"], 1)
            pe.wait_ge(sem["selg_ready"], total1)
            gates_of_block(bank_d, False).then_inc(sem["comb_psum"], 1)
            pe.wait_ge(sem["yb1_ready"], total1)
            pe.wait_ge(sem["comb_ready"], total1)
            scatter(0)
            scatter(1).then_inc(sem["scattered"], 1)

        @block.scalar
        def _(act):
            def fn(out_, in_, func, **kw):
                return nc.scalar.activation(out_, in_, func, **kw)

            def rows_squared(src, i, t, signal):
                fn(squares, src[:, t, :], ACT.Square, accum_out=ssq[:, i + t:i + t + 1]).then_inc(signal, 1)
                act.wait_ge(signal, t + 1)

            roots = [0]

            def root_guess(dst, mean):
                roots[0] += 1
                act.wait_ge(sem["mean_ready"], roots[0])
                fn(dst, mean, ACT.Ln).then_inc(sem["root_ln"], 1)
                act.wait_ge(sem["root_ln"], roots[0])
                fn(dst, dst, ACT.Exp, scale=-0.5).then_inc(sem["root_guess"], 1)

            def row_norm(i, t):
                root_guess(rstd[:, i + t:i + t + 1], ssq[:, i + t:i + t + 1])

            def take(job, dst, src=None, **kw):
                wait_full(act, job)
                src = bank_of(job)[:, :] if src is None else src
                taken(fn(dst, src, ACT.Copy, **kw), job)

            def tiles(job, n):
                return bank_of(job)[:, :].rearrange("p (k t) -> p k t", t=n)

            for t in range(NT):
                act.wait_ge(sem["x_in"], 32)
                rows_squared(x_res, 0, t, sem["x_squared"])
            for t in range(NT):
                row_norm(0, t)
            act.wait_ge(sem["mem_in"], 16)
            for t in range(NT):
                rows_squared(mem_raw, 2, t, sem["mem_squared"])
            for t in range(NT):
                row_norm(2, t)
            act.wait_ge(sem["lb_diff"], 1)
            fn(lb2[:, 0, :], lb2[:, 1, :], ACT.Exp).then_inc(sem["lb_exp"], 1)
            for t in range(NT):
                wait_full(act, f"hf{t}")
                taken(fn(e_f[:, t, :], bank_of(f"hf{t}")[:, :], ACT.Exp, scale=-1.0), f"hf{t}")
            take("glr", glrT, bank_of("glr")[0:RANK, 0:T])
            act.wait_ge(sem["z_abs"], 1)
            fn(ez, ez, ACT.Exp).then_inc(sem["z_exp"], 1)
            act.wait_ge(sem["z_exp"], 1)
            fn(l_z, ez, ACT.Ln, bias=1.0).then_inc(sem["z_ln"], 1)
            for t in range(NT):
                act.wait_ge(sem["f_ready"], t + 1)
                fn(g_tok[:, t, 0:512], f_tok[:, t, :], ACT.Ln).then_inc(sem["lnf_ready"], 1)
            for i in range(2):
                wait_full(act, f"hq{i}")
                fn(tmp[:, i, :], bank_of(f"hq{i}")[:, :], ACT.Exp, scale=-1.0).then_inc(sem["hq_exp"], 1)
            for i in range(3):
                take(f"b{i}", bT[:, 2 * i:2 * i + 2, :], tiles(f"b{i}", T), scale=1.0 if i < 2 else 1.0 / GATE_NORM)
            take("gq", qT[:, 4:6, :], tiles("gq", T), scale=GKD ** -0.5)
            take("gk", kT[:, 4:6, :], tiles("gk", T))

            def decay(n):
                act.wait_ge(sem["r_diff"], n + 1)
                fn(R[:, n % 2], R[:, n % 2], ACT.Exp).then_inc(sem["r_exp"], 1)

            def gate_exp(name, i):
                for t in range(NT):
                    if i == 0:
                        wait_taken(act, f"hq{t}")
                    else:
                        act.wait_ge(sem["gate_ready"], t + 1)
                    wait_full(act, f"{name}{t}")
                    fn(tmp[:, t, :], bank_of(f"{name}{t}")[:, :], ACT.Exp, scale=-1.0).then_inc(sem["gate_exp"], 1)

            decay(0)
            decay(1)
            take("hi0", v_tok[:, 0, 0:512])
            take("hi1", v_tok[:, 1, 0:512])
            decay(2)
            take("gv0", v_tok[:, 0, 512:1024])
            take("gv1", v_tok[:, 1, 512:1024])
            decay(3)
            gate_exp("hg", 0)
            decay(4)
            gate_exp("gg", 1)
            decay(5)
            take("xk0", xkT[:, 0:2, :], tiles("xk0", T))
            take("xk1", xkT[:, 2:4, :], tiles("xk1", T))
            decay(6)
            take("xk2", xkT[:, 4:6, :], tiles("xk2", T))
            take("xk3", xkT[:, 6:8, :], tiles("xk3", T))
            decay(7)
            act.wait_ge(sem["gate_ready"], 4)
            for t in range(NT):
                take(f"xv0{t}", xv0[:, t, :])
            take("lv128_h0", S[:, 0:HEADS, 2, :], tiles("lv128_h0", P))
            for half in range(2):
                take(f"lv128_g{half}", S_gla(half)[:, :, 2, :], tiles(f"lv128_g{half}", P)[:, 0:2, :])
            take("diag", stat[:, 32:48], bank_of("diag")[:, 0:16])
            for t in range(NT):
                root_guess(hrms[:, t, :], hsq[:, t, :])
            take("xv10", xv1[:, 0, :])
            for t in range(NT):
                for h in range(2):
                    take(f"yT{t}{h}", yT[:, 4 * h:4 * h + 4, t * P:(t + 1) * P], tiles(f"yT{t}{h}", P))
            for t in range(NT):
                for h in range(2):
                    wait_taken(act, f"out{h}{t}")
                rows_squared(x_res, 4, t, sem["x1_squared"])
            for t in range(NT):
                row_norm(4, t)
            take("xv11", xv1[:, 1, :])
            for j in range(4):
                take(f"xq{j}", qxT[:, 2 * j:2 * j + 2, :], tiles(f"xq{j}", T), scale=(D // XH) ** -0.5)
            for t in range(NT):
                for h in range(2):
                    job = f"sc{t}{h}"
                    act.wait_ge(sem["neg_max"], 2 * t + h + 1)
                    for i in range(2):
                        a = 2 * h + i
                        ins = fn(probs[:, t, a, :], bank_of(job)[:, i * T:(i + 1) * T], ACT.Exp,
                                 bias=nmax[:, t, a:a + 1], accum_out=psums[:, t, a:a + 1])
                    taken(ins, job)
            for h in range(XH):
                take(f"pT{h}", probsT[:, h], tiles(f"pT{h}", T))
            for h in range(XH):
                take(f"pv{h}", oT[:, 2 * h:2 * h + 2, :], tiles(f"pv{h}", T))
            for t in range(NT):
                for h in range(2):
                    wait_taken(act, f"xo{h}{t}")
                rows_squared(x_res, 6, t, sem["x2_squared"])
            for t in range(NT):
                row_norm(6, t)
            take("bias", biasT.rearrange("p e m -> p m e"), tiles("bias", E))
            for t in range(NT):
                for h in range(2):
                    take(f"eT{t}{h}", h2T[:, 4 * h:4 * h + 4, t * P:(t + 1) * P], tiles(f"eT{t}{h}", P))
            for t in range(NT):
                act.wait_ge(sem["gate_max"], 1)
                fn(gate_ex[:, t, :], logits[:, t, :], ACT.Exp, bias=ngmax[:, t:t + 1]).then_inc(sem["gate_exps"], 1)
            take("gT", gT_sb, bank_of("gT")[0:E, 0:T])

            wait_taken(act, "table")
            with act.Fori(0, E) as e:
                blocks = act.value_load(table[0:1, bass.ds(e, 1)], min_val=1, max_val=MAXB)
                first = act.value_load(table[0:1, bass.ds(e + E, 1)], min_val=0, max_val=MAXB * E)
                with act.Fori(0, blocks) as c:
                    w1 = act.snap(first + c + 1)
                    act.wait_ge(sem["xb_psum"], w1)
                    fn(xbT, bank_a[:, :].rearrange("p (k r) -> p k r", r=ROWS), ACT.Copy).then_inc(sem["xb_ready"], 1)
                    act.wait_ge(sem["yb0_psum"], w1)
                    fn(yb[:, 0:512], bank_d[0:ROWS, :], ACT.Copy).then_inc(sem["yb0_ready"], 1)
                    act.wait_ge(sem["comb_psum"], w1)
                    fn(combT, bank_d[0:ROWS, 0:T], ACT.Copy).then_inc(sem["comb_ready"], 1)
                    act.wait_ge(sem["yb1_psum"], w1)
                    fn(yb[:, 512:1024], bank_a[0:ROWS, :], ACT.Copy).then_inc(sem["yb1_ready"], 1)
                    act.wait_ge(sem["g_clamped"], w1)
                    fn(sg_t, g_t, ACT.Sigmoid, scale=ALPHA).then_inc(sem["sig_ready"], 1)
                    act.wait_ge(sem["chunk_used"], act.snap(CHUNKS * w1))
                    fn(yT_sb, bank_d[:, :].rearrange("p (k r) -> p k r", r=ROWS), ACT.Copy).then_inc(sem["yT_ready"], 1)
            total1 = act.snap(act.value_load(table[0:1, 3 * E:3 * E + 1], min_val=E, max_val=MAXB * E) + 1)
            act.wait_ge(sem["yb1_psum"], total1)
            fn(yb[:, 0:512], bank_a[0:ROWS, :], ACT.Copy).then_inc(sem["yb0_ready"], 1)
            fn(yb[:, 512:1024], bank_g[0:ROWS, :], ACT.Copy).then_inc(sem["yb1_ready"], 1)
            act.wait_ge(sem["comb_psum"], total1)
            fn(combT, bank_d[0:ROWS, 0:T], ACT.Copy).then_inc(sem["comb_ready"], 1)
            for t in range(NT):
                act.wait_ge(sem["out_summed"], 2 * t + 2)
                rows_squared(x_res, 0, t, sem["out_squared"])
            for t in range(NT):
                row_norm(0, t)

        @block.vector
        def _(dve):
            v = nc.vector
            steps = [0]

            def link(ins):
                steps[0] += 1
                ins.then_inc(sem["dve_step"], 1)
                dve.wait_ge(sem["dve_step"], steps[0])

            def tiles(job, n):
                return bank_of(job)[:, :].rearrange("p (k t) -> p k t", t=n)

            roots = [0]

            def inv_rms(dst, src, n):
                roots[0] += 1
                v.tensor_scalar(src, src, 1.0 / n, EPS, ALU.mult, ALU.add).then_inc(sem["mean_ready"], 1)
                dve.wait_ge(sem["root_guess"], roots[0])
                t = newton[:, 0:src.shape[1]]
                link(v.tensor_tensor(t, src, dst, ALU.mult))
                link(v.tensor_tensor(t, t, dst, ALU.mult))
                link(v.tensor_scalar(t, t, -0.5, 1.5, ALU.mult, ALU.add))
                link(v.tensor_tensor(dst, dst, t, ALU.mult))

            def normalise(src, i, squared, signal):
                for t in range(NT):
                    dve.wait_ge(squared, t + 1)
                    inv_rms(rstd[:, i + t:i + t + 1], ssq[:, i + t:i + t + 1], D)
                    v.tensor_scalar(xn[:, t, :], src[:, t, :], rstd[:, i + t:i + t + 1], None, ALU.mult).then_inc(signal, 1)

            def weigh(prefix, dst, w):
                for t in range(NT):
                    for h in range(2):
                        job = f"{prefix}{t}{h}"
                        wait_full(dve, job)
                        taken(v.tensor_tensor(dst[:, 4 * h:4 * h + 4, t * P:(t + 1) * P], tiles(job, P),
                                              w[:, 4 * h:4 * h + 4].unsqueeze(2).broadcast_to([P, 4, P]), ALU.mult), job)

            def over_one_plus(dst, num, ex):
                link(v.tensor_scalar(ex, ex, 1.0, None, ALU.add))
                link(v.reciprocal(ex, ex))
                return v.tensor_tensor(dst, num, ex, ALU.mult)

            normalise(x_res, 0, sem["x_squared"], sem["x_normed"])
            dve.wait_ge(sem["w_mix_in"], 16)
            weigh("xT", hT, w_mix)
            dve.wait_ge(sem["lb_in"], 16)
            v.tensor_tensor(lb2[:, 1, :], lb2[:, 1, :], lb2[:, 0, :], ALU.subtract).then_inc(sem["lb_diff"], 1)
            normalise(mem_raw, 2, sem["mem_squared"], sem["mem_normed"])
            dve.wait_ge(sem["lb_exp"], 1)
            link(v.tensor_scalar(lb2[:, 0, :], lb2[:, 0, :], 1.0, None, ALU.add))
            link(v.reciprocal(lb2[:, 0, :], lb2[:, 0, :]))
            link(v.tensor_scalar(lb2[:, 1, :], lb2[:, 0, :], -1.0, 1.0, ALU.mult, ALU.add))
            for t in range(NT):
                wait_taken(dve, f"hf{t}")
                link(over_one_plus(f_tok[:, t, :], lb2[:, 1, :], e_f[:, t, :]))
                v.tensor_tensor(f_tok[:, t, :], f_tok[:, t, :], lb2[:, 0, :], ALU.add).then_inc(sem["f_ready"], 1)
            dve.wait_ge(sem["gk_bias_in"], 16)
            wait_full(dve, "z")
            ins = v.tensor_tensor(zb, tiles("z", 256), gk_bias.unsqueeze(1).broadcast_to([P, NT, 256]), ALU.add)
            taken(ins, "z")
            wait_taken(dve, "z")
            v.scalar_tensor_tensor(ez, zb, -1.0, zb, ALU.mult, ALU.min).then_inc(sem["z_abs"], 1)
            dve.wait_ge(sem["vec_in"], 64)
            weigh("mT", memT, w_mem)
            dve.wait_ge(sem["z_ln"], 1)
            v.scalar_tensor_tensor(g_tok[:, :, 512:768], zb, 0.0, l_z, ALU.min, ALU.subtract).then_inc(sem["g_ready"], 1)
            for i in range(2):
                dve.wait_ge(sem["hq_exp"], i + 1)
                taken(over_one_plus(qT[:, 2 * i:2 * i + 2, :], tiles(f"hq{i}", T), tmp[:, i, :].rearrange("p (k t) -> p k t", t=T)), f"hq{i}")
            for i in range(2):
                wait_full(dve, f"fT{i}")
                taken(v.tensor_scalar(kT[:, 2 * i:2 * i + 2, :], tiles(f"fT{i}", T), -1.0, 1.0, ALU.mult, ALU.add), f"fT{i}")

            def halves(m, s):
                mm = m.rearrange("p k (b a r) -> p (k b) a r", a=2, r=s)
                return mm[:, :, 0, :], mm[:, :, 1, :]

            def by_chunk(m):
                return m.rearrange("p k (c r) -> p k c r", r=CHUNK)

            def differences(n):
                s = LEVELS[n]
                Rn = R[:, n % 2]
                if n >= 2:
                    for job in level_jobs(LEVELS[n - 2]):
                        wait_full(dve, job)
                if s < CHUNK:
                    b1, b2 = halves(bT, s)
                    r1, r2 = halves(Rn, s)
                    last = b1[:, :, s - 1:s].broadcast_to(list(b1.shape))
                    v.tensor_tensor(r1, last, b1, ALU.subtract)
                    v.tensor_tensor(r2, b2, last, ALU.subtract).then_inc(sem["r_diff"], 1)
                    return
                b, r = by_chunk(bT), by_chunk(Rn)
                ends = b[:, :, :, CHUNK - 1:CHUNK]

                def end_of(c):
                    return ends[:, :, c, :].broadcast_to([P, QT, CHUNK])

                if s == CHUNK:
                    for c in (0, 2):
                        v.tensor_tensor(r[:, :, c, :], end_of(c), b[:, :, c, :], ALU.subtract)
                        ins = v.tensor_copy(r[:, :, c + 1, :], b[:, :, c + 1, :])
                else:
                    v.tensor_tensor(r[:, :, 1, :], end_of(1), b[:, :, 1, :], ALU.subtract)
                    v.tensor_copy(r[:, :, 2, :], b[:, :, 2, :])
                    v.tensor_tensor(r[:, :, 3, :], b[:, :, 3, :], end_of(2), ALU.add)
                    link(v.tensor_tensor(r[:, :, 0, :], end_of(0), b[:, :, 0, :], ALU.subtract))
                    ins = v.tensor_tensor(r[:, :, 0, :], r[:, :, 0, :], end_of(1), ALU.add)
                ins.then_inc(sem["r_diff"], 1)

            def decayed(n):
                s = LEVELS[n]
                r1, r2 = halves(R[:, n % 2], s)
                k1, _ = halves(kT, s)
                _, q2 = halves(qT, s)
                dve.wait_ge(sem["r_exp"], n + 1)
                v.tensor_tensor(r1, r1, k1, ALU.mult)
                v.tensor_tensor(r2, r2, q2, ALU.mult).then_inc(sem["r_ready"], 1)

            def take_scores(n):
                s = LEVELS[n]
                mask = masks[:, n, :].bitcast(I32)
                for t in range(NT):
                    job = f"lv{s}_h{t}"
                    wait_full(dve, job)
                    taken(v.copy_predicated(S[:, 0:HEADS, t, :], mask.unsqueeze(1).broadcast_to([P, HEADS, P]), tiles(job, P)), job)
                for half in range(2):
                    job = f"lv{s}_g{half}"
                    wait_full(dve, job)
                    src = bank_of(job)[:, :].rearrange("p (h t i) -> p h t i", h=2, t=NT)
                    taken(v.copy_predicated(S_gla(half)[:, :, 0:NT, :],
                                            mask.unsqueeze(1).unsqueeze(1).broadcast_to([P, 2, NT, P]), src), job)

            def gate(name, g):
                for t in range(NT):
                    job = f"{name}{t}"
                    dve.wait_ge(sem["gate_exp"], 2 * g + t + 1)
                    dst = gates[:, t, g * 512:(g + 1) * 512]
                    taken(over_one_plus(dst, bank_of(job)[:, :], tmp[:, t, :]), job)
                    wait_taken(dve, job)
                    d4 = dst.rearrange("p (h n) -> p h n", n=VD)
                    v.tensor_tensor(d4, d4, onorm[:, g * VD:(g + 1) * VD].unsqueeze(1).broadcast_to([P, HEADS, VD]),
                                    ALU.mult).then_inc(sem["gate_ready"], 1)

            for job in ("b0", "b1", "b2"):
                wait_taken(dve, job)
            differences(0)
            differences(1)
            for job in ("gq", "gk", "hq0", "hq1", "fT0", "fT1"):
                wait_taken(dve, job)
            decayed(0)
            decayed(1)
            dve.wait_ge(sem["s_zeroed"], 1)
            dve.wait_ge(sem["masks_ready"], len(LEVELS) - 1)
            for n in range(7):
                if n in (2, 3):
                    gate(("hg", "gg")[n - 2], n - 2)
                take_scores(n)
                if n + 2 < 8:
                    differences(n + 2)
                    decayed(n + 2)
            v.tensor_tensor(R[:, 0], qT, kT, ALU.mult).then_inc(sem["r_ready"], 1)

            wait_taken(dve, "diag")
            for t in range(NT):
                for g, group in enumerate("hg"):
                    job = f"o{t}{group}"
                    wait_full(dve, job)
                    for h in range(HEADS):
                        hh = g * HEADS + h
                        ins = v.scalar_tensor_tensor(o_tok[:, t, hh * VD:(hh + 1) * VD], v_tok[:, t, hh * VD:(hh + 1) * VD],
                                                     dots[:, t, hh:hh + 1], bank_of(job)[:, h * VD:(h + 1) * VD], ALU.mult, ALU.add)
                    taken(ins, job)
                    wait_taken(dve, job)
                ot = o_tok[:, t, :]
                o8 = ot.rearrange("p (h n) -> p h n", n=VD)
                link(v.tensor_tensor(xn[:, t, :], ot, ot, ALU.mult))
                link(v.tensor_reduce(hsq[:, t, :], xn[:, t, :].rearrange("p (h n) -> p h n", n=VD), AX.X, ALU.add))
                inv_rms(hrms[:, t, :], hsq[:, t, :], VD)
                link(v.tensor_tensor(o8, o8, hrms[:, t, :].unsqueeze(2).broadcast_to([P, 2 * HEADS, VD]), ALU.mult))
                v.tensor_tensor(ot, ot, gates[:, t, :], ALU.mult).then_inc(sem["y_ready"], 1)

            def add_rows(prefix):
                for h in range(2):
                    for t in range(NT):
                        job = f"{prefix}{h}{t}"
                        wait_full(dve, job)
                        dst = x_res[:, t, h * 512:(h + 1) * 512]
                        taken(v.tensor_tensor(dst, dst, bank_of(job)[:, :], ALU.add), job)

            add_rows("out")
            normalise(x_res, 4, sem["x1_squared"], sem["x1_normed"])
            weigh("aT", aT, w_xa)
            for t in range(NT):
                for h in range(2):
                    wait_full(dve, f"sc{t}{h}")
                    v.tensor_reduce(nmax[:, t, 2 * h:2 * h + 2], tiles(f"sc{t}{h}", T), AX.X, ALU.max,
                                    negate=True).then_inc(sem["neg_max"], 1)
            for t in range(NT):
                for h in range(2):
                    wait_taken(dve, f"sc{t}{h}")
                    r = psums[:, t, 2 * h:2 * h + 2]
                    link(v.reciprocal(r, r))
                    p2 = probs[:, t, 2 * h:2 * h + 2, :]
                    v.tensor_tensor(p2, p2, r.unsqueeze(2).broadcast_to([P, 2, T]), ALU.mult).then_inc(sem["p_ready"], 1)
            add_rows("xo")
            dve.wait_ge(sem["moe_row_in"], 16)
            for t in range(NT):
                dve.wait_ge(sem["x2_squared"], t + 1)
                inv_rms(rstd[:, 6 + t:7 + t], ssq[:, 6 + t:7 + t], D)
                v.scalar_tensor_tensor(h2[:, t, :], x_res[:, t, :], rstd[:, 6 + t:7 + t], norm_row, ALU.mult,
                                       ALU.mult).then_inc(sem["h2_ready"], 1)
            dve.wait_ge(sem["router_in"], 32)
            wait_full(dve, "router")
            taken(v.tensor_tensor(logits, bank_of("router")[:, 0:NT * E].rearrange("p (t e) -> p t e", e=E),
                                  b_router.unsqueeze(1).broadcast_to([P, NT, E]), ALU.add), "router")
            wait_taken(dve, "router")
            for t in range(NT):
                link(v.max(top8[:, t, :], logits[:, t, :]))
            v.tensor_scalar(ngmax, top8[:, :, 0], -1.0, None, ALU.mult).then_inc(sem["gate_max"], 1)
            for t in range(NT):
                link(v.max_index(idx8[:, t * 8:(t + 1) * 8], top8[:, t, :], logits[:, t, :]))
            link(v.tensor_copy(idxf, idx8[:, :].rearrange("p (t e) -> p t e", t=NT)))
            for r in range(TOPK):
                for t in range(NT):
                    if r == 0:
                        ins = v.tensor_scalar(chosen[:, t, :], iota[:, 0:E], idxf[:, t, r:r + 1], None, ALU.is_equal)
                    else:
                        ins = v.scalar_tensor_tensor(chosen[:, t, :], iota[:, 0:E], idxf[:, t, r:r + 1], chosen[:, t, :],
                                                     ALU.is_equal, ALU.add)
                    if (r, t) != (TOPK - 1, NT - 1):
                        link(ins)
            ins.then_inc(sem["chosen_ready"], 1)
            dve.wait_ge(sem["chosen_ready"], 1)
            v.memset(yT_sb, 0.0).then_inc(sem["yT_ready"], 1)
            v.memset(selg, 0.0).then_inc(sem["selg_ready"], 1)
            dve.wait_ge(sem["gate_exps"], NT)
            link(v.tensor_tensor(gate_tok, gate_ex, chosen, ALU.mult))
            link(v.tensor_reduce(gsum, gate_tok, AX.X, ALU.add))
            link(v.reciprocal(gsum, gsum))
            v.tensor_tensor(gate_tok, gate_tok, gsum.unsqueeze(2).broadcast_to([P, NT, E]), ALU.mult).then_inc(sem["gates_ready"], 1)
            wait_full(dve, "count")
            count = bank_of("count")[0:E, 0:1]
            link(v.tensor_scalar(nb_col, count, float(ROWS), 1.0, ALU.is_gt, ALU.add))
            for m in range(2, MAXB):
                ins = v.scalar_tensor_tensor(nb_col, count, float(m * ROWS), nb_col, ALU.is_gt, ALU.add)
                if m < MAXB - 1:
                    link(ins)
            taken(ins, "count")
            wait_full(dve, "rank")
            ins = v.scalar_tensor_tensor(rank_m, bank_of("rank")[:, 0:NT * E].rearrange("p (t e) -> p t e", e=E), 1.0, chosen,
                                         ALU.add, ALU.mult)
            taken(ins, "rank")
            wait_taken(dve, "rank")
            link(v.tensor_scalar(rank_m, rank_m, -1.0, None, ALU.add))
            wait_full(dve, "table")
            rows = bank_of("table")[0:1, 0:2 * E]
            link(v.tensor_copy(table_f[0:1, 0:2 * E], rows))
            v.tensor_copy(table[0:1, 0:2 * E], table_f[0:1, 0:2 * E])
            link(v.tensor_scalar(table_f[0:1, 2 * E:3 * E], table_f[0:1, E:2 * E], float(CHUNKS), -float(CHUNKS), ALU.mult, ALU.add))
            v.tensor_scalar(table[0:1, 2 * E:3 * E], table_f[0:1, 2 * E:3 * E], 0.0, None, ALU.max)
            taken(v.tensor_tensor(table[0:1, 3 * E:3 * E + 1], table_f[0:1, E - 1:E], table_f[0:1, 2 * E - 1:2 * E], ALU.add), "table")
            wait_taken(dve, "table")
            wait_taken(dve, "bias")

            with dve.Fori(0, E) as e:
                blocks = dve.value_load(table[0:1, bass.ds(e, 1)], min_val=1, max_val=MAXB)
                first = dve.value_load(table[0:1, bass.ds(e + E, 1)], min_val=0, max_val=MAXB * E)
                with dve.Fori(0, blocks) as c:
                    w0 = dve.snap(first + c)
                    w1 = dve.snap(first + c + 1)
                    rows = iota[:, bass.ds(c * ROWS, ROWS)]
                    for t in range(NT):
                        ins = v.tensor_scalar(sel[:, t, :], rows, rank_m[:, t, bass.ds(e, 1)], None, ALU.is_equal)
                    ins.then_inc(sem["sel_ready"], 1)
                    dve.wait_ge(sem["gate_done"], w1)
                    v.tensor_tensor(g_t, bank_g[:, :].rearrange("p (k r) -> p k r", r=ROWS),
                                    biasT[:, bass.ds(e, 1), 0:8].rearrange("p o m -> p (o m)").unsqueeze(2).broadcast_to([P, 8, ROWS]),
                                    ALU.add).then_inc(sem["swiglu_step"], 1)
                    base = dve.snap(w0 * 3)
                    dve.wait_ge(sem["swiglu_step"], base + 1)
                    v.tensor_scalar(g_t, g_t, LIMIT, None, ALU.min).then_inc(sem["g_clamped"], 1)
                    dve.wait_ge(sem["chunk_used"], CHUNKS * w0 + GU_CHUNKS)
                    v.tensor_tensor(u_t, bank_u[:, :].rearrange("p (k r) -> p k r", r=ROWS),
                                    biasT[:, bass.ds(e, 1), 8:16].rearrange("p o m -> p (o m)").unsqueeze(2).broadcast_to([P, 8, ROWS]),
                                    ALU.add).then_inc(sem["swiglu_step"], 1)
                    dve.wait_ge(sem["swiglu_step"], base + 2)
                    v.tensor_scalar(u_t, u_t, LIMIT, -LIMIT, ALU.min, ALU.max).then_inc(sem["swiglu_step"], 1)
                    dve.wait_ge(sem["swiglu_step"], base + 3)
                    dve.wait_ge(sem["g_clamped"], w1)
                    v.scalar_tensor_tensor(u_t, u_t, 1.0, g_t, ALU.add, ALU.mult).then_inc(sem["up_gated"], 1)
                    dve.wait_ge(sem["up_gated"], w1)
                    dve.wait_ge(sem["sig_ready"], w1)
                    v.tensor_tensor(act_t, u_t, sg_t, ALU.mult).then_inc(sem["act_ready"], 1)
                    for t in range(NT):
                        ins = v.tensor_scalar(selg[:, t, :], rows, rank_m[:, t, bass.ds(e, 1)], gate_tok[:, t, bass.ds(e, 1)],
                                              ALU.is_equal, ALU.mult)
                    ins.then_inc(sem["selg_ready"], 1)
            dve.wait_ge(sem["scattered"], 1)
            for t in range(NT):
                for h in range(2):
                    dst = x_res[:, t, h * 512:(h + 1) * 512]
                    v.tensor_tensor(dst, dst, bank_y[t][h][:, :], ALU.add).then_inc(sem["out_summed"], 1)
            dve.wait_ge(sem["final_row_in"], 16)
            for t in range(NT):
                dve.wait_ge(sem["out_squared"], t + 1)
                inv_rms(rstd[:, t:t + 1], ssq[:, t:t + 1], D)
                v.scalar_tensor_tensor(xn[:, t, :], x_res[:, t, :], rstd[:, t:t + 1], norm_row, ALU.mult,
                                       ALU.mult).then_inc(sem["out_ready"], 1)


_INS = ["x", "mem", "norm_mix_w", "w_in", "hg_lb_logits", "hg_onorm_w", "gla_w_gk2", "gla_b_gk", "gla_onorm_w", "w_out",
        "norm_xa_w", "norm_mem_w", "w_xq", "w_xkv", "w_xo", "norm_moe_w", "w_router", "b_router", "w_gate_up",
        "b_gate_up", "w_down", "b_down", "norm_final_w"]


def kernel(**inputs):
    import concourse.bacc as bacc
    from concourse.bass_utils import run_bass_kernel_spmd

    nc = bacc.Bacc("TRN2", target_bir_lowering=False, num_devices=1)
    arrays, aps = {}, {}
    for name in _INS:
        a = np.ascontiguousarray(inputs[name])
        arrays[f"in_{name}"] = a
        aps[name] = nc.dram_tensor(f"in_{name}", a.shape, mybir.dt.from_np(a.dtype), kind="ExternalInput").ap()
    out = nc.dram_tensor("out_0", (1, T, D), F32, kind="ExternalOutput").ap()
    build(nc, aps, out)
    result = run_bass_kernel_spmd(nc, [arrays], core_ids=[0])
    return result.results[0]["out_0"]
```

```python
from contextlib import ExitStack

import numpy as np

import concourse.bass as bass
from concourse import mybir

F32 = mybir.dt.float32
BF16 = mybir.dt.bfloat16
I32 = mybir.dt.int32
U32 = mybir.dt.uint32
ALU = mybir.AluOpType
ACT = mybir.ActivationFunctionType
AX = mybir.AxisListType

P = 128
D = 1024
T = 256
NT = T // P
KT = D // P
EPS = 1e-6
CHUNK = 64
VD = 128
HEADS = 4
QT = 6
GKD = 64
RANK = 16
GATE_NORM = 16.0
C_HQ, C_HF, C_HI, C_HG, C_GQ, C_GV, C_GG, C_GLR = 0, 512, 1024, 1536, 2048, 2560, 3072, 3584
XH = 4
E = 32
TOPK = 4
LIMIT = 7.0
ALPHA = 1.702
ROWS = 64
MAXB = T // ROWS
CHUNKS = 12
GU_CHUNKS = KT
PW = 512
SLOTS = 6


PANELS = [("w_in", C_HF, "hf1"), ("w_in", C_HQ, "hq1"), ("w_in", C_GQ, "gk"), ("w_in", C_HI, "hi1"),
          ("w_in", C_GV, "gv1"), ("w_in", C_HG, "hg1"), ("w_in", C_GG, "gg1"), ("w_xkv", 0, "xk1"),
          ("w_xkv", PW, "xk3"), ("w_xkv", 2 * PW, "xv01"), ("w_out", 0, "out01"), ("w_out", PW, "out11"),
          ("w_xkv", 3 * PW, "xv11"), ("w_xq", 0, "xq1"), ("w_xq", PW, "xq3"), ("w_xo", 0, "xo01"), ("w_xo", PW, "xo11")]
LEVELS = [1, 2, 4, 8, 16, 32, 64, 128]


def four(name):
    return [f"{name}{t}{h}" for t in range(2) for h in range(2)]


def level_jobs(s):
    return [f"lv{s}_h{t}" for t in range(NT if s < P else 1)] + [f"lv{s}_g{half}" for half in range(2)]


JOBS = (four("xT") + ["hf0", "hf1", "glr", "z"] + four("mT") + ["hq0", "hq1", "fT0", "fT1", "b0", "b1", "b2", "gq", "gk"]
        + ["hi0", "hi1"] + level_jobs(1) + ["gv0", "gv1"] + level_jobs(2) + ["hg0", "hg1"] + level_jobs(4)
        + ["gg0", "gg1"] + level_jobs(8) + ["xk0", "xk1"] + level_jobs(16) + ["xk2"] + level_jobs(32)
        + level_jobs(64) + ["xv00", "xv01"] + level_jobs(128) + ["diag", "o0h", "o0g", "o1h", "o1g", "xv10"]
        + four("yT") + four("out") + ["xk3"] + four("aT") + ["xq0", "xq1", "xq2", "xq3"]
        + ["sc00", "sc10", "sc01", "sc11", "xv11", "pT0", "pT1", "pT2", "pT3", "pv0", "pv1", "pv2", "pv3"] + four("xo") + four("eT")
        + ["router", "rank", "count", "table", "gT"])

SEMS = """w_mix_in mem_in vec_in lb_in glr_in gk_bias_in router_in moe_row_in final_row_in bias_in
 consts_ready masks_ready s_zeroed x_squared x_normed mem_squared mem_normed lb_diff lb_sigmoid f_ready lnf_ready
 z_abs z_exp z_ln g_ready hq_sigmoid k_ready r_diff r_exp r_ready gate_sigmoid gate_ready y_ready x1_squared x1_normed
 neg_max p_exp p_ready x2_squared h2_ready gate_max gate_exps chosen_ready nb_ready gates_ready up_gated part_ready rest_ready
 dve_step pool_step sel_ready xb_psum xb_ready comb_psum comb_ready gate_done
 g_clamped u_clamped sig_ready act_ready selg_ready chunk_used actT_psum actT_ready yb_ready
 scattered out_summed out_squared out_ready stored""".split()


def build(nc, A, out):
    ctx = ExitStack()
    with ctx:
        ctx.enter_context(nc.allow_non_contiguous_dma("small vectors are laid out by feature"))

        def sb(name, cols, dt=F32, rows=P):
            return ctx.enter_context(nc.sbuf_tensor(name, [rows, cols], dt))

        sem = {n: ctx.enter_context(nc.semaphore(n)) for n in SEMS}
        bank_full = [ctx.enter_context(nc.semaphore(f"bank_full{b}")) for b in range(8)]
        bank_taken = [ctx.enter_context(nc.semaphore(f"bank_taken{b}")) for b in range(8)]
        x_in = [ctx.enter_context(nc.semaphore(f"x_in{t}")) for t in range(NT)]
        panel_in = [ctx.enter_context(nc.semaphore(f"panel_in{s}")) for s in range(SLOTS)]
        chunk_in = [ctx.enter_context(nc.semaphore(f"chunk_in{k}")) for k in range(CHUNKS)]
        banks = [ctx.enter_context(nc.psum_tensor(f"bank{b}", [P, 512], F32)) for b in range(8)]

        ring = sb("ring", CHUNKS * 2048)
        x_res_t = sb("x_res", NT * D)
        region1 = sb("region1", KT * T)
        region2 = sb("region2", KT * T)
        region3 = sb("region3", KT * T)
        region5 = sb("region5", NT * D)
        region6 = sb("region6", NT * D)
        region7 = sb("region7", 3 * QT * T)
        region10 = sb("region10", NT * D)
        r_t = sb("r_levels", 2 * QT * T)
        s_t = sb("s_matrices", 2 * HEADS * 3 * P)
        tmp_t = sb("tmp", 1024)
        row_t = sb("rows", 1024)
        ident = sb("ident", P)
        tri = sb("tri", P)
        strict = sb("strict", P)
        ones = sb("ones", P)
        iota = sb("iota", T)
        onorm = sb("onorm", 2 * VD)
        cols = sb("norm_cols", 3 * KT)
        stat = sb("stat", 88)
        idx8 = sb("idx8", NT * 8, U32)
        table = sb("table", 3 * E + 1, I32, rows=1)

        def fm(t, off=0):
            return t[:, off:off + KT * T].rearrange("p (k t) -> p k t", t=T)

        def tm(t, off=0, n=D):
            return t[:, off:off + NT * n].rearrange("p (t n) -> p t n", n=n)

        small = region1
        x_res = tm(x_res_t)
        hT, yT, aT, oT = fm(region1), fm(region1), fm(region1), fm(region1)
        memT, h2T = fm(region2), fm(region2)
        f_tok = tm(region3, 0, 512)
        zb = tm(region3, 1024, 256)
        ez = tm(region3, 1536, 256)
        xkT = fm(region3)
        b_gu = region3[:, 0:2 * D]
        mem_raw, v_tok = tm(region5), tm(region5)
        probs = region5[:, :].rearrange("p (t h m) -> p t h m", t=NT, h=XH)
        b_down_sb = region5[0:E, 0:D]
        lb2 = region6[:, 0:1024].rearrange("p (a n) -> p a n", a=2)
        squares = region6[:, 1024:2048]
        gates = tm(region6)
        rest = tm(region6)
        probsT = region6[:, :].rearrange("p (h m t) -> p h m t", h=XH, m=2)
        qT = region7[:, 0:1536].rearrange("p (k t) -> p k t", t=T)
        kT = region7[:, 1536:3072].rearrange("p (k t) -> p k t", t=T)
        bT = region7[:, 3072:4608].rearrange("p (k t) -> p k t", t=T)
        w_glr = region7[:, 3072:3200].rearrange("p (k n) -> p k n", n=RANK)
        gk2 = region7[0:RANK, 3200:3456]
        glrT = region7[0:RANK, 3456:3712]
        sel = region7[:, 0:NT * ROWS // 2].bitcast(BF16).rearrange("p (t r) -> p t r", t=NT)
        one_hot = region7[:, 64:64 + ROWS]
        selg = region7[:, 128:384].rearrange("p (t r) -> p t r", t=NT)
        combT = region7[:, 384:640]
        xbT, actT = (region7[:, c:c + KT * ROWS].rearrange("p (k r) -> p k r", r=ROWS) for c in (640, 1152))
        act_t, g_t, u_t, sg_t, yb = (region7[:, c:c + 512] for c in range(1664, 4224, 512))
        w_router = region7[:, 1024:1280].rearrange("p (k n) -> p k n", n=E)
        b_router = region7[:, 1280:1280 + E]
        gT_sb = region7[0:E, 1536:1536 + T]
        xn, h2 = tm(region10), tm(region10)
        R = r_t[:, :].rearrange("p (a k t) -> p a k t", a=2, t=T)
        qxT = fm(r_t)
        h2_parts = r_t[:, :].bitcast(BF16).rearrange("p (i t n) -> p i t n", i=3, t=NT)
        o_tok = r_t[:, 0:NT * D].rearrange("p (t n) -> p t n", n=D)
        S = s_t[:, :].rearrange("p (h a i) -> p h a i", h=2 * HEADS, a=3)

        def S_gla(half):
            return S[:, HEADS + half::2, :, :]

        g_tok = tm(s_t, 0, 768)
        sig_f = tm(s_t, 1536, 512)
        l_z = tm(s_t, 2560, 256)
        xv0, xv1 = tm(tmp_t, 0, 512), tm(s_t, 0, 512)
        tmp = tmp_t[:, :].rearrange("p (a n) -> p a n", a=2)
        gk_bias = tmp_t[:, 0:256]
        masks = row_t[:, 0:(len(LEVELS) - 1) * P].rearrange("p (l i) -> p l i", i=P)
        norm_row = row_t[:, :]
        w_mix, w_xa, w_mem = (cols[:, i * KT:(i + 1) * KT] for i in range(3))
        rstd = stat[:, 0:8]
        ssq = stat[:, 8:16]
        hsq = stat[:, 16:32].rearrange("p (t h) -> p t h", t=NT)
        hrms = stat[:, 64:80].rearrange("p (t h) -> p t h", t=NT)
        newton = stat[:, 80:88]
        dots = stat[:, 32:48].rearrange("p (t h) -> p t h", t=NT)
        nmax = stat[:, 48:56].rearrange("p (t h) -> p t h", t=NT)
        psums = stat[:, 56:64].rearrange("p (t h) -> p t h", t=NT)
        logits, chosen, gate_ex, gate_tok, rank_m = (small[:, c:c + NT * E].rearrange("p (t e) -> p t e", t=NT)
                                                     for c in range(0, 320, 64))
        top8, idxf = (small[:, c:c + NT * 8].rearrange("p (t e) -> p t e", t=NT) for c in (320, 336))
        gsum, ngmax, nb_col = small[:, 352:354], small[:, 354:356], small[0:E, 356:357]
        table_f = small[0:1, 360:360 + 3 * E]

        def panel(n):
            s = n % SLOTS
            return ring[:, s * 4096:(s + 1) * 4096].rearrange("p (k n) -> p k n", n=PW)

        def chunk(k):
            return ring[:, k * 2048:(k + 1) * 2048]

        def bank_of(job):
            return banks[JOBS.index(job) % 8]

        def wait_full(eng, job):
            n = JOBS.index(job)
            eng.wait_ge(bank_full[n % 8], n // 8 + 1)

        def wait_taken(eng, job):
            n = JOBS.index(job)
            eng.wait_ge(bank_taken[n % 8], n // 8 + 1)

        def taken(ins, job):
            ins.then_inc(bank_taken[JOBS.index(job) % 8], 1)

        bank_y = [[banks[0], banks[1]], [banks[2], banks[3]]]
        bank_a, bank_g, bank_u, bank_d = banks[4], banks[5], banks[6], banks[7]
        block = ctx.enter_context(nc.Block())

        def by_feature(v):
            return v.rearrange("(k p) -> p k", p=P)

        @block.sync
        def _(sp):
            for t in range(NT):
                sp.dma_start(x_res[:, t, :], A["x"][0, t * P:(t + 1) * P, :]).then_inc(x_in[t], 16)
            sp.dma_start(w_mix, by_feature(A["norm_mix_w"][0])).then_inc(sem["w_mix_in"], 16)
            weight = {"w_in": A["w_in"], "w_xkv": A["w_xkv"], "w_out": A["w_out"], "w_xq": A["w_xq"], "w_xo": A["w_xo"]}
            for n, (name, c0, _) in enumerate(PANELS):
                if n >= SLOTS:
                    wait_full(sp, PANELS[n - SLOTS][2])
                src = weight[name][0, :, c0:c0 + PW].rearrange("(k p) n -> p k n", p=P)
                sp.dma_start(panel(n), src).then_inc(panel_in[n % SLOTS], 16)
                if n == 0:
                    sp.dma_start(lb2, A["hg_lb_logits"].rearrange("(o a) n -> o a n", o=1).broadcast_to([P, 2, 512])).then_inc(sem["lb_in"], 16)
                    sp.dma_start(w_glr, A["w_in"][0, :, C_GLR:C_GLR + RANK].rearrange("(k p) n -> p k n", p=P)).then_inc(sem["glr_in"], 16)
                    sp.dma_start(gk2, A["gla_w_gk2"][0]).then_inc(sem["glr_in"], 16)
                    sp.dma_start(gk_bias, A["gla_b_gk"].broadcast_to([P, 256])).then_inc(sem["gk_bias_in"], 16)
                    sp.dma_start(mem_raw, A["mem"][0].rearrange("(t p) n -> p t n", p=P)).then_inc(sem["mem_in"], 16)

            def load_chunk(e, k):
                if k < GU_CHUNKS:
                    src = A["w_gate_up"][0, e, k * P:(k + 1) * P, :]
                    dst = chunk(k)
                else:
                    j = k - GU_CHUNKS
                    src = A["w_down"][0, e, 2 * j * P:(2 * j + 2) * P, :].rearrange("(a p) n -> p a n", p=P)
                    dst = chunk(k).rearrange("p (a n) -> p a n", a=2)
                sp.dma_start(dst, src).then_inc(chunk_in[k], 16)

            for n in sorted(range(len(PANELS) - SLOTS, len(PANELS)), key=lambda n: JOBS.index(PANELS[n][2])):
                wait_full(sp, PANELS[n][2])
                for k in (2 * (n % SLOTS), 2 * (n % SLOTS) + 1):
                    load_chunk(0, k)
            wait_taken(sp, "table")
            with sp.Fori(1, E) as e:
                used = sp.value_load(table[0:1, bass.ds(e + 2 * E, 1)], min_val=0, max_val=CHUNKS * MAXB * E)
                for k in range(CHUNKS):
                    sp.wait_ge(sem["chunk_used"], used + (k + 1))
                    load_chunk(e, k)
            for t in range(NT):
                sp.wait_ge(sem["out_ready"], t + 1)
                sp.dma_start(out[0, t * P:(t + 1) * P, :], xn[:, t, :]).then_inc(sem["stored"], 16)
            sp.wait_ge(sem["stored"], 16 * NT)

        @block.gpsimd
        def _(pool):
            steps = [0]

            def link(ins):
                steps[0] += 1
                ins.then_inc(sem["pool_step"], 1)
                pool.wait_ge(sem["pool_step"], steps[0])

            link(pool.memset(ident[:, :], 0.0))
            link(pool.affine_select(out=ident[:, :], in_=ident[:, :], compare_op=ALU.not_equal, fill=1.0, base=0,
                                    pattern=[[-1, P]], channel_multiplier=1))
            link(pool.memset(ones[:, :], 1.0))
            link(pool.affine_select(out=tri[:, :], in_=ones[:, :], compare_op=ALU.is_ge, fill=0.0, base=0,
                                    pattern=[[1, P]], channel_multiplier=-1))
            link(pool.memset(tri[0:CHUNK, CHUNK:P], 0.0))
            link(pool.affine_select(out=strict[:, :], in_=ones[:, :], compare_op=ALU.is_gt, fill=0.0, base=0,
                                    pattern=[[1, P]], channel_multiplier=-1))
            pool.iota(iota[:, :], pattern=[[1, T]], base=0, channel_multiplier=0,
                      allow_small_or_imprecise_dtypes=True).then_inc(sem["consts_ready"], 1)
            pool.dma_start(w_mem, by_feature(A["norm_mem_w"][0])).then_inc(sem["vec_in"], 16)
            pool.dma_start(w_xa, by_feature(A["norm_xa_w"][0])).then_inc(sem["vec_in"], 16)
            pool.dma_start(onorm[:, 0:VD], A["hg_onorm_w"].broadcast_to([P, VD])).then_inc(sem["vec_in"], 16)
            pool.dma_start(onorm[:, VD:2 * VD], A["gla_onorm_w"].broadcast_to([P, VD])).then_inc(sem["vec_in"], 16)
            for n, s in enumerate(LEVELS[:-1]):
                m = masks[:, n, :].rearrange("p (b a r) -> p b a r", a=2, r=s)
                link(pool.memset(masks[:, n, :], 0.0))
                link(pool.memset(m[:, :, 1, :], 1.0))
                link(pool.affine_select(out=m[:, :, 1, :], in_=m[:, :, 1, :], compare_op=ALU.is_ge, fill=0.0, base=0,
                                        pattern=[[-2 * s, P // (2 * s)], [0, s]], channel_multiplier=1))
                pool.affine_select(out=m[:, :, 1, :], in_=m[:, :, 1, :], compare_op=ALU.is_gt, fill=0.0, base=s,
                                   pattern=[[2 * s, P // (2 * s)], [0, s]], channel_multiplier=-1).then_inc(sem["masks_ready"], 1)
            for job in ("b0", "b1", "b2"):
                wait_full(pool, job)
            pool.memset(s_t[:, :], 0.0).then_inc(sem["s_zeroed"], 1)
            wait_full(pool, "diag")
            pool.dma_start(w_router, A["w_router"][0].rearrange("(k p) n -> p k n", p=P)).then_inc(sem["router_in"], 16)
            pool.dma_start(b_router, A["b_router"].broadcast_to([P, E])).then_inc(sem["router_in"], 16)
            for job in level_jobs(64):
                wait_taken(pool, job)
            pool.dma_start(norm_row, A["norm_moe_w"].broadcast_to([P, D])).then_inc(sem["moe_row_in"], 16)
            wait_full(pool, "sc11")
            link(pool.memset(b_gu, 0.0))
            pool.dma_start(b_gu[0:E, :], A["b_gate_up"][0]).then_inc(sem["bias_in"], 16)
            wait_full(pool, "pT3")
            pool.dma_start(b_down_sb, A["b_down"][0]).then_inc(sem["bias_in"], 16)
            for i, src in enumerate((h2, rest)):
                pool.wait_ge(sem["h2_ready"] if i == 0 else sem["rest_ready"], NT if i == 0 else 1)
                pool.wait_ge(sem["part_ready"], i + 1)
                pool.tensor_tensor(rest, src, h2_parts[:, i], ALU.subtract).then_inc(sem["rest_ready"], 1)
            pool.dma_start(norm_row, A["norm_final_w"].rearrange("(o n) -> o n", o=1).broadcast_to([P, D])).then_inc(sem["final_row_in"], 16)

        @block.tensor
        def _(pe):
            done = [0]

            def begin(job):
                n = done[0]
                assert JOBS[n] == job, (JOBS[n], job)
                if n >= 8:
                    wait_taken(pe, JOBS[n - 8])
                return banks[n % 8]

            def end(ins):
                ins.then_inc(bank_full[done[0] % 8], 1)
                done[0] += 1

            def arrived(first_job_weight, c0):
                n = [p[:2] for p in PANELS].index((first_job_weight, c0))
                pe.wait_ge(panel_in[n % SLOTS], 16 * (n // SLOTS + 1))
                return panel(n)

            def transposes(prefix, src):
                for t in range(NT):
                    for h in range(2):
                        bk = begin(f"{prefix}{t}{h}")
                        for i in range(4):
                            k = 4 * h + i
                            last = pe.transpose(bk[:, i * P:(i + 1) * P], src[:, t, k * P:(k + 1) * P], ident[:, :])
                        end(last)

            def by_feature(job, w, m, rhs):
                bk = begin(job)
                for i in range(2):
                    for k in range(KT):
                        last = pe.matmul(bk[:, i * T:(i + 1) * T], w[:, k, (m + i) * P:(m + i + 1) * P], rhs[:, k, :],
                                         start=(k == 0), stop=(k == KT - 1))
                end(last)

            def by_token(job, w, t, lhs):
                bk = begin(job)
                for k in range(KT):
                    last = pe.matmul(bk[:, :], lhs[:, k, t * P:(t + 1) * P], w[:, k, :], start=(k == 0), stop=(k == KT - 1))
                end(last)

            def level(n):
                pe.wait_ge(sem["r_ready"], n + 1)
                s = LEVELS[n]
                tiles = [(t, t) for t in range(NT)] if s < P else [(0, 1)]

                def scores(out_, rows, j, i):
                    return pe.matmul(out_, rows[:, j * P:(j + 1) * P], rows[:, i * P:(i + 1) * P], start=True, stop=True)

                for j, i in tiles:
                    bk = begin(f"lv{s}_h{j}")
                    for h in range(HEADS):
                        last = scores(bk[:, h * P:(h + 1) * P], R[:, n % 2, h, :], j, i)
                    end(last)
                for half in range(2):
                    bk = begin(f"lv{s}_g{half}")
                    for h in range(2):
                        rows = R[GKD * half:GKD * (half + 1), n % 2, HEADS + h, :]
                        for a, (j, i) in enumerate(tiles):
                            c = (h * len(tiles) + a) * P
                            last = scores(bk[:, c:c + P], rows, j, i)
                    end(last)

            pe.wait_ge(sem["consts_ready"], 1)
            pe.wait_ge(sem["x_normed"], NT)
            transposes("xT", xn)
            for job in four("xT"):
                wait_taken(pe, job)
            w = arrived("w_in", C_HF)
            by_token("hf0", w, 0, hT)
            by_token("hf1", w, 1, hT)
            pe.wait_ge(sem["glr_in"], 32)
            bk = begin("glr")
            for k in range(KT):
                last = pe.matmul(bk[0:RANK, 0:T], w_glr[:, k, :], hT[:, k, :], start=(k == 0), stop=(k == KT - 1))
            end(last)
            wait_taken(pe, "glr")
            bk = begin("z")
            for t in range(NT):
                last = pe.matmul(bk[:, t * 256:(t + 1) * 256], glrT[:, t * P:(t + 1) * P], gk2, start=True, stop=True)
            end(last)
            pe.wait_ge(sem["mem_normed"], NT)
            transposes("mT", xn)
            w = arrived("w_in", C_HQ)
            by_feature("hq0", w, 0, hT)
            by_feature("hq1", w, 2, hT)
            pe.wait_ge(sem["f_ready"], NT)
            for i in range(2):
                bk = begin(f"fT{i}")
                for a in range(2):
                    for t in range(NT):
                        last = pe.transpose(bk[:, a * T + t * P:a * T + (t + 1) * P],
                                            f_tok[:, t, (2 * i + a) * P:(2 * i + a + 1) * P], ident[:, :])
                end(last)
            pe.wait_ge(sem["lnf_ready"], NT)
            pe.wait_ge(sem["g_ready"], 1)
            for i in range(3):
                bk = begin(f"b{i}")
                for a in range(2):
                    for t in range(NT):
                        last = pe.matmul(bk[:, a * T + t * P:a * T + (t + 1) * P],
                                         g_tok[:, t, (2 * i + a) * P:(2 * i + a + 1) * P], tri[:, :], start=True, stop=True)
                end(last)
            w = arrived("w_in", C_GQ)
            by_feature("gq", w, 0, hT)
            by_feature("gk", w, 2, hT)
            for n, (name, c0) in enumerate((("hi", C_HI), ("gv", C_GV), ("hg", C_HG), ("gg", C_GG))):
                w = arrived("w_in", c0)
                by_token(f"{name}0", w, 0, hT)
                by_token(f"{name}1", w, 1, hT)
                level(n)
            for job in four("mT"):
                wait_taken(pe, job)
            w = arrived("w_xkv", 0)
            by_feature("xk0", w, 0, memT)
            by_feature("xk1", w, 2, memT)
            level(4)
            by_feature("xk2", arrived("w_xkv", PW), 0, memT)
            level(5)
            level(6)
            w = arrived("w_xkv", 2 * PW)
            by_token("xv00", w, 0, memT)
            by_token("xv01", w, 1, memT)
            level(7)
            pe.wait_ge(sem["r_ready"], 9)
            bk = begin("diag")
            for k in range(QT):
                for t in range(NT):
                    if k < HEADS:
                        c, n, rhs = t * 2 * HEADS + k, 1, ones[:, 0:1]
                    else:
                        c, n, rhs = t * 2 * HEADS + HEADS + 2 * (k - HEADS), 2, tri[:, CHUNK - 1::CHUNK]
                    last = pe.matmul(bk[:, c:c + n], R[:, 0, k, t * P:(t + 1) * P], rhs, start=True, stop=True)
            end(last)
            for job in level_jobs(64) + level_jobs(128) + ["hi0", "hi1", "gv0", "gv1"]:
                wait_taken(pe, job)
            for t in range(NT):
                for g, group in enumerate("hg"):
                    bk = begin(f"o{t}{group}")
                    for h in range(HEADS):
                        hh = g * HEADS + h
                        parts = [(0, 0)] if t == 0 else [(2, 0), (1, 1)]
                        for a, j in parts:
                            last = pe.matmul(bk[:, h * VD:(h + 1) * VD], S[:, hh, a, :], v_tok[:, j, hh * VD:(hh + 1) * VD],
                                             start=(j == 0), stop=(j == t))
                    end(last)
            w = arrived("w_xkv", 3 * PW)
            by_token("xv10", w, 0, memT)
            for t in range(NT):
                pe.wait_ge(sem["y_ready"], t + 1)
                for h in range(2):
                    bk = begin(f"yT{t}{h}")
                    for i in range(4):
                        k = 4 * h + i
                        last = pe.transpose(bk[:, i * P:(i + 1) * P], o_tok[:, t, k * P:(k + 1) * P], ident[:, :])
                    end(last)
            for job in four("yT"):
                wait_taken(pe, job)
            for i in range(2):
                w = arrived("w_out", i * PW)
                by_token(f"out{i}0", w, 0, yT)
                by_token(f"out{i}1", w, 1, yT)
            by_feature("xk3", arrived("w_xkv", PW), 2, memT)
            pe.wait_ge(sem["x1_normed"], NT)
            transposes("aT", xn)
            for job in four("aT"):
                wait_taken(pe, job)
            for i in range(2):
                w = arrived("w_xq", i * PW)
                by_feature(f"xq{2 * i}", w, 0, aT)
                by_feature(f"xq{2 * i + 1}", w, 2, aT)
            for job in ["xk0", "xk1", "xk2", "xk3", "xq0", "xq1", "xq2", "xq3"]:
                wait_taken(pe, job)
            for h in range(2):
                for t in range(NT):
                    bk = begin(f"sc{t}{h}")
                    for i in range(2):
                        for a in range(2):
                            k = 2 * (2 * h + i) + a
                            last = pe.matmul(bk[:, i * T:(i + 1) * T], qxT[:, k, t * P:(t + 1) * P], xkT[:, k, :],
                                             start=(a == 0), stop=(a == 1))
                    end(last)
            by_token("xv11", arrived("w_xkv", 3 * PW), 1, memT)
            for h in range(XH):
                pe.wait_ge(sem["p_ready"], 2 * (h // 2) + 2)
                bk = begin(f"pT{h}")
                for m in range(2):
                    for t in range(NT):
                        last = pe.transpose(bk[:, m * T + t * P:m * T + (t + 1) * P], probs[:, t, h, m * P:(m + 1) * P], ident[:, :])
                end(last)
            for job in ["xv00", "xv01", "xv10", "xv11"]:
                wait_taken(pe, job)
            for h in range(XH):
                wait_taken(pe, f"pT{h}")
                bk = begin(f"pv{h}")
                for a in range(2):
                    c = (2 * (h % 2) + a) * P
                    for m in range(2):
                        last = pe.matmul(bk[:, a * T:(a + 1) * T], (xv0, xv1)[h // 2][:, m, c:c + P], probsT[:, h, m, :],
                                         start=(m == 0), stop=(m == 1))
                end(last)
            for h in range(XH):
                wait_taken(pe, f"pv{h}")
            for i in range(2):
                w = arrived("w_xo", i * PW)
                by_token(f"xo{i}0", w, 0, oT)
                by_token(f"xo{i}1", w, 1, oT)
            pe.wait_ge(sem["h2_ready"], NT)
            transposes("eT", h2)
            for job in four("eT"):
                wait_taken(pe, job)
            pe.wait_ge(sem["router_in"], 32)
            bk = begin("router")
            for t in range(NT):
                for k in range(KT):
                    last = pe.matmul(bk[:, t * E:(t + 1) * E], h2T[:, k, t * P:(t + 1) * P], w_router[:, k, :],
                                     start=(k == 0), stop=(k == KT - 1))
            end(last)
            pe.wait_ge(sem["chosen_ready"], 1)
            bk = begin("rank")
            pe.matmul(bk[:, 0:E], strict[:, :], chosen[:, 0, :], start=True, stop=True)
            pe.matmul(bk[:, E:2 * E], ones[:, :], chosen[:, 0, :], start=True, stop=False)
            end(pe.matmul(bk[:, E:2 * E], strict[:, :], chosen[:, 1, :], start=False, stop=True))
            bk = begin("count")
            pe.matmul(bk[0:E, 0:1], chosen[:, 0, :], ones[:, 0:1], start=True, stop=False)
            end(pe.matmul(bk[0:E, 0:1], chosen[:, 1, :], ones[:, 0:1], start=False, stop=True))
            wait_taken(pe, "count")
            bk = begin("table")
            pe.matmul(bk[0:1, 0:E], nb_col, ident[0:E, 0:E], start=True, stop=True)
            end(pe.matmul(bk[0:1, E:2 * E], nb_col, strict[0:E, 0:E], start=True, stop=True))
            pe.wait_ge(sem["gates_ready"], 1)
            bk = begin("gT")
            for t in range(NT):
                last = pe.transpose(bk[0:E, t * P:(t + 1) * P], gate_tok[:, t, :], ident[:, :])
            end(last)

            for job in JOBS[-8:]:
                wait_taken(pe, job)
            pe.wait_ge(sem["part_ready"], 3)
            pe.wait_ge(sem["bias_in"], 32)
            for t in range(NT):
                for h in range(2):
                    pe.matmul(bank_y[t][h][:, :], gT_sb[:, t * P:(t + 1) * P], b_down_sb[:, h * 512:(h + 1) * 512],
                              start=True, stop=False, skip_group_check=True)

            def pair(bk, lhs, w, start, stop):
                for half in range(2):
                    last = pe.matmul(bk[half * ROWS:(half + 1) * ROWS, :], lhs, w[:, half * 512:(half + 1) * 512],
                                     start=start, stop=stop, skip_group_check=True)
                return last

            def scatter():
                for t in range(NT):
                    for half in range(2):
                        rows = slice(half * ROWS, (half + 1) * ROWS)
                        last = pe.matmul(bank_y[t][half][:, :], combT[rows, t * P:(t + 1) * P], yb[rows, :],
                                         start=False, stop=False, skip_group_check=True)
                return last

            with pe.Fori(0, E) as e:
                blocks = pe.value_load(table[0:1, bass.ds(e, 1)], min_val=1, max_val=MAXB)
                first = pe.value_load(table[0:1, bass.ds(e + E, 1)], min_val=0, max_val=MAXB * E)
                in_e = pe.snap(16 * e + 16)
                with pe.Fori(0, blocks) as c:
                    w1 = pe.snap(first + c + 1)
                    pe.wait_ge(sem["sel_ready"], w1)
                    for k in range(KT):
                        for i in range(3):
                            for t in range(NT):
                                last = pe.matmul(bank_a[:, k * ROWS:(k + 1) * ROWS], h2_parts[:, i, t, k * P:(k + 1) * P],
                                                 sel[:, t, :], start=(i == 0 and t == 0), stop=(i == 2 and t == NT - 1),
                                                 skip_group_check=True)
                    last.then_inc(sem["xb_psum"], 1)
                    for bk, c0 in ((bank_g, 0), (bank_u, D)):
                        pair(bk, one_hot, b_gu[:, c0:c0 + D], True, False)
                    pe.wait_ge(sem["xb_ready"], w1)
                    for k in range(GU_CHUNKS):
                        pe.wait_ge(chunk_in[k], in_e)
                        wk = chunk(k)
                        last = pair(bank_g, xbT[:, k, :], wk[:, 0:D], False, k == KT - 1)
                        if k == KT - 1:
                            last.then_inc(sem["gate_done"], 1)
                        pair(bank_u, xbT[:, k, :], wk[:, D:2 * D], False, k == KT - 1).then_inc(sem["chunk_used"], 1)
                    pe.wait_ge(sem["yb_ready"], w1)
                    scatter()
                    pe.wait_ge(sem["selg_ready"], w1)
                    for t in range(NT):
                        last = pe.matmul(bank_d[:, t * P:(t + 1) * P], selg[:, t, :], ident[:, :], start=True, stop=True,
                                         is_transpose=True, skip_group_check=True)
                    last.then_inc(sem["comb_psum"], 1)
                    pe.wait_ge(sem["act_ready"], w1)
                    for i in range(4):
                        last = pe.matmul(bank_a[:, i * P:(i + 1) * P], act_t[:, i * P:(i + 1) * P], ident[:, :], start=True,
                                         stop=True, is_transpose=True, skip_group_check=True)
                    last.then_inc(sem["actT_psum"], 1)
                    pe.wait_ge(sem["comb_ready"], w1)
                    pe.wait_ge(sem["actT_ready"], w1)
                    for j in range(CHUNKS - GU_CHUNKS):
                        pe.wait_ge(chunk_in[GU_CHUNKS + j], in_e)
                        for a in range(2):
                            f = 2 * j + a
                            last = pair(bank_d, actT[:, f, :], chunk(GU_CHUNKS + j)[:, a * D:(a + 1) * D], f == 0, f == KT - 1)
                        last.then_inc(sem["chunk_used"], 1)
            total = pe.value_load(table[0:1, 3 * E:3 * E + 1], min_val=E, max_val=MAXB * E)
            pe.wait_ge(sem["yb_ready"], pe.snap(total + 1))
            scatter().then_inc(sem["scattered"], 1)

        @block.scalar
        def _(act):
            def fn(out_, in_, func, **kw):
                return nc.scalar.activation(out_, in_, func, **kw)

            def rows_squared(src, i, t, signal):
                fn(squares, src[:, t, :], ACT.Square, accum_out=ssq[:, i + t:i + t + 1]).then_inc(signal, 1)
                act.wait_ge(signal, t + 1)

            def take(job, dst, src=None, **kw):
                wait_full(act, job)
                src = bank_of(job)[:, :] if src is None else src
                taken(fn(dst, src, ACT.Copy, **kw), job)

            def tiles(job, n):
                return bank_of(job)[:, :].rearrange("p (k t) -> p k t", t=n)

            for t in range(NT):
                act.wait_ge(x_in[t], 16)
                rows_squared(x_res, 0, t, sem["x_squared"])
            act.wait_ge(sem["mem_in"], 16)
            for t in range(NT):
                rows_squared(mem_raw, 2, t, sem["mem_squared"])
            act.wait_ge(sem["lb_diff"], 1)
            fn(lb2[:, 0, :], lb2[:, 0, :], ACT.Sigmoid).then_inc(sem["lb_sigmoid"], 1)
            for t in range(NT):
                wait_full(act, f"hf{t}")
                taken(fn(sig_f[:, t, :], bank_of(f"hf{t}")[:, :], ACT.Sigmoid), f"hf{t}")
            take("glr", glrT, bank_of("glr")[0:RANK, 0:T])
            act.wait_ge(sem["z_abs"], 1)
            fn(ez, ez, ACT.Exp).then_inc(sem["z_exp"], 1)
            act.wait_ge(sem["z_exp"], 1)
            fn(l_z, ez, ACT.Ln, bias=1.0).then_inc(sem["z_ln"], 1)
            for t in range(NT):
                act.wait_ge(sem["f_ready"], t + 1)
                fn(g_tok[:, t, 0:512], f_tok[:, t, :], ACT.Ln).then_inc(sem["lnf_ready"], 1)
            for i in range(2):
                wait_full(act, f"hq{i}")
                fn(tmp[:, i, :], bank_of(f"hq{i}")[:, :], ACT.Sigmoid).then_inc(sem["hq_sigmoid"], 1)
            for i in range(3):
                take(f"b{i}", bT[:, 2 * i:2 * i + 2, :], tiles(f"b{i}", T), scale=1.0 if i < 2 else 1.0 / GATE_NORM)
            take("gq", qT[:, 4:6, :], tiles("gq", T), scale=GKD ** -0.5)
            take("gk", kT[:, 4:6, :], tiles("gk", T))

            def decay(n):
                act.wait_ge(sem["r_diff"], n + 1)
                fn(R[:, n % 2], R[:, n % 2], ACT.Exp).then_inc(sem["r_exp"], 1)

            def gate_sigmoid(name, i):
                for t in range(NT):
                    if i == 0:
                        wait_taken(act, f"hq{t}")
                    else:
                        act.wait_ge(sem["gate_ready"], t + 1)
                    wait_full(act, f"{name}{t}")
                    fn(tmp[:, t, :], bank_of(f"{name}{t}")[:, :], ACT.Sigmoid).then_inc(sem["gate_sigmoid"], 1)

            decay(0)
            decay(1)
            take("hi0", v_tok[:, 0, 0:512])
            take("hi1", v_tok[:, 1, 0:512])
            decay(2)
            take("gv0", v_tok[:, 0, 512:1024])
            take("gv1", v_tok[:, 1, 512:1024])
            decay(3)
            gate_sigmoid("hg", 0)
            decay(4)
            gate_sigmoid("gg", 1)
            decay(5)
            take("xk0", xkT[:, 0:2, :], tiles("xk0", T))
            take("xk1", xkT[:, 2:4, :], tiles("xk1", T))
            decay(6)
            take("xk2", xkT[:, 4:6, :], tiles("xk2", T))
            decay(7)
            act.wait_ge(sem["gate_ready"], 4)
            for t in range(NT):
                take(f"xv0{t}", xv0[:, t, :])
            take("lv128_h0", S[:, 0:HEADS, 2, :], tiles("lv128_h0", P))
            for half in range(2):
                take(f"lv128_g{half}", S_gla(half)[:, :, 2, :], tiles(f"lv128_g{half}", P)[:, 0:2, :])
            take("diag", stat[:, 32:48], bank_of("diag")[:, 0:16])
            take("xv10", xv1[:, 0, :])
            for t in range(NT):
                for h in range(2):
                    take(f"yT{t}{h}", yT[:, 4 * h:4 * h + 4, t * P:(t + 1) * P], tiles(f"yT{t}{h}", P))
            for t in range(NT):
                for h in range(2):
                    wait_taken(act, f"out{h}{t}")
                rows_squared(x_res, 4, t, sem["x1_squared"])
            take("xk3", xkT[:, 6:8, :], tiles("xk3", T))
            for j in range(4):
                take(f"xq{j}", qxT[:, 2 * j:2 * j + 2, :], tiles(f"xq{j}", T), scale=(D // XH) ** -0.5)
            for h in range(2):
                for t in range(NT):
                    job = f"sc{t}{h}"
                    act.wait_ge(sem["neg_max"], 2 * h + t + 1)
                    for i in range(2):
                        a = 2 * h + i
                        ins = fn(probs[:, t, a, :], bank_of(job)[:, i * T:(i + 1) * T], ACT.Exp,
                                 bias=nmax[:, t, a:a + 1], accum_out=psums[:, t, a:a + 1])
                    taken(ins, job)
            take("xv11", xv1[:, 1, :])
            for h in range(XH):
                take(f"pT{h}", probsT[:, h], tiles(f"pT{h}", T))
            for h in range(XH):
                take(f"pv{h}", oT[:, 2 * h:2 * h + 2, :], tiles(f"pv{h}", T))
            for t in range(NT):
                for h in range(2):
                    wait_taken(act, f"xo{h}{t}")
                rows_squared(x_res, 6, t, sem["x2_squared"])
            for t in range(NT):
                for h in range(2):
                    take(f"eT{t}{h}", h2T[:, 4 * h:4 * h + 4, t * P:(t + 1) * P], tiles(f"eT{t}{h}", P))
            for i, src in enumerate((h2, rest, rest)):
                if i:
                    act.wait_ge(sem["rest_ready"], i)
                fn(h2_parts[:, i], src, ACT.Copy).then_inc(sem["part_ready"], 1)
            for t in range(NT):
                act.wait_ge(sem["gate_max"], 1)
                fn(gate_ex[:, t, :], logits[:, t, :], ACT.Exp, bias=ngmax[:, t:t + 1]).then_inc(sem["gate_exps"], 1)
            take("gT", gT_sb, bank_of("gT")[0:E, 0:T])

            wait_taken(act, "table")
            with act.Fori(0, E) as e:
                blocks = act.value_load(table[0:1, bass.ds(e, 1)], min_val=1, max_val=MAXB)
                first = act.value_load(table[0:1, bass.ds(e + E, 1)], min_val=0, max_val=MAXB * E)
                with act.Fori(0, blocks) as c:
                    w1 = act.snap(first + c + 1)
                    act.wait_ge(sem["xb_psum"], w1)
                    fn(xbT, bank_a[:, :].rearrange("p (k r) -> p k r", r=ROWS), ACT.Copy).then_inc(sem["xb_ready"], 1)
                    act.wait_ge(sem["g_clamped"], w1)
                    fn(sg_t, g_t, ACT.Sigmoid, scale=ALPHA).then_inc(sem["sig_ready"], 1)
                    act.wait_ge(sem["comb_psum"], w1)
                    fn(combT, bank_d[:, 0:T], ACT.Copy).then_inc(sem["comb_ready"], 1)
                    act.wait_ge(sem["actT_psum"], w1)
                    fn(actT.rearrange("p (h i) r -> p i h r", h=2), bank_a[:, :].rearrange("p (i h r) -> p i h r", h=2, r=ROWS),
                       ACT.Copy).then_inc(sem["actT_ready"], 1)
                    act.wait_ge(sem["chunk_used"], act.snap(CHUNKS * w1))
                    fn(yb, bank_d[:, :], ACT.Copy).then_inc(sem["yb_ready"], 1)
            for t in range(NT):
                act.wait_ge(sem["out_summed"], 2 * t + 2)
                rows_squared(x_res, 0, t, sem["out_squared"])

        @block.vector
        def _(dve):
            v = nc.vector
            steps = [0]

            def link(ins):
                steps[0] += 1
                ins.then_inc(sem["dve_step"], 1)
                dve.wait_ge(sem["dve_step"], steps[0])

            def tiles(job, n):
                return bank_of(job)[:, :].rearrange("p (k t) -> p k t", t=n)

            def inv_rms(dst, src, n):
                t = newton[:, 0:src.shape[1]]
                link(v.tensor_scalar(src, src, 1.0 / n, EPS, ALU.mult, ALU.add))
                link(v.tensor_scalar(dst.bitcast(I32), src.bitcast(I32), 1, None, ALU.arith_shift_right))
                link(v.tensor_scalar(dst.bitcast(I32), dst.bitcast(I32), -1.0, float(0x5F3759DF), ALU.mult, ALU.add))
                for _ in range(3):
                    link(v.tensor_tensor(t, src, dst, ALU.mult))
                    link(v.tensor_tensor(t, t, dst, ALU.mult))
                    link(v.tensor_scalar(t, t, -0.5, 1.5, ALU.mult, ALU.add))
                    link(v.tensor_tensor(dst, dst, t, ALU.mult))

            def normalise(src, i, squared, signal):
                dve.wait_ge(squared, NT)
                inv_rms(rstd[:, i:i + NT], ssq[:, i:i + NT], D)
                for t in range(NT):
                    v.tensor_scalar(xn[:, t, :], src[:, t, :], rstd[:, i + t:i + t + 1], None, ALU.mult).then_inc(signal, 1)

            def weigh(prefix, dst, w):
                for t in range(NT):
                    for h in range(2):
                        job = f"{prefix}{t}{h}"
                        wait_full(dve, job)
                        taken(v.tensor_tensor(dst[:, 4 * h:4 * h + 4, t * P:(t + 1) * P], tiles(job, P),
                                              w[:, 4 * h:4 * h + 4].unsqueeze(2).broadcast_to([P, 4, P]), ALU.mult), job)

            normalise(x_res, 0, sem["x_squared"], sem["x_normed"])
            dve.wait_ge(sem["w_mix_in"], 16)
            weigh("xT", hT, w_mix)
            dve.wait_ge(sem["lb_in"], 16)
            v.tensor_tensor(lb2[:, 0, :], lb2[:, 0, :], lb2[:, 1, :], ALU.subtract).then_inc(sem["lb_diff"], 1)
            normalise(mem_raw, 2, sem["mem_squared"], sem["mem_normed"])
            dve.wait_ge(sem["lb_sigmoid"], 1)
            link(v.tensor_scalar(lb2[:, 1, :], lb2[:, 0, :], -1.0, 1.0, ALU.mult, ALU.add))
            for t in range(NT):
                wait_taken(dve, f"hf{t}")
                link(v.tensor_tensor(f_tok[:, t, :], lb2[:, 1, :], sig_f[:, t, :], ALU.mult))
                v.tensor_tensor(f_tok[:, t, :], f_tok[:, t, :], lb2[:, 0, :], ALU.add).then_inc(sem["f_ready"], 1)
            dve.wait_ge(sem["gk_bias_in"], 16)
            wait_full(dve, "z")
            ins = v.tensor_tensor(zb, tiles("z", 256), gk_bias.unsqueeze(1).broadcast_to([P, NT, 256]), ALU.add)
            taken(ins, "z")
            wait_taken(dve, "z")
            v.scalar_tensor_tensor(ez, zb, -1.0, zb, ALU.mult, ALU.min).then_inc(sem["z_abs"], 1)
            dve.wait_ge(sem["vec_in"], 64)
            weigh("mT", memT, w_mem)
            dve.wait_ge(sem["z_ln"], 1)
            v.scalar_tensor_tensor(g_tok[:, :, 512:768], zb, 0.0, l_z, ALU.min, ALU.subtract).then_inc(sem["g_ready"], 1)
            for i in range(2):
                dve.wait_ge(sem["hq_sigmoid"], i + 1)
                taken(v.tensor_tensor(qT[:, 2 * i:2 * i + 2, :], tiles(f"hq{i}", T),
                                      tmp[:, i, :].rearrange("p (k t) -> p k t", t=T), ALU.mult), f"hq{i}")
            for i in range(2):
                wait_full(dve, f"fT{i}")
                taken(v.tensor_scalar(kT[:, 2 * i:2 * i + 2, :], tiles(f"fT{i}", T), -1.0, 1.0, ALU.mult, ALU.add), f"fT{i}")

            def halves(m, s):
                mm = m.rearrange("p k (b a r) -> p (k b) a r", a=2, r=s)
                return mm[:, :, 0, :], mm[:, :, 1, :]

            def by_chunk(m):
                return m.rearrange("p k (c r) -> p k c r", r=CHUNK)

            def differences(n):
                s = LEVELS[n]
                Rn = R[:, n % 2]
                if n >= 2:
                    for job in level_jobs(LEVELS[n - 2]):
                        wait_full(dve, job)
                if s < CHUNK:
                    b1, b2 = halves(bT, s)
                    r1, r2 = halves(Rn, s)
                    last = b1[:, :, s - 1:s].broadcast_to(list(b1.shape))
                    v.tensor_tensor(r1, last, b1, ALU.subtract)
                    v.tensor_tensor(r2, b2, last, ALU.subtract).then_inc(sem["r_diff"], 1)
                    return
                b, r = by_chunk(bT), by_chunk(Rn)
                ends = b[:, :, :, CHUNK - 1:CHUNK]

                def end_of(c):
                    return ends[:, :, c, :].broadcast_to([P, QT, CHUNK])

                if s == CHUNK:
                    for c in (0, 2):
                        v.tensor_tensor(r[:, :, c, :], end_of(c), b[:, :, c, :], ALU.subtract)
                        ins = v.tensor_copy(r[:, :, c + 1, :], b[:, :, c + 1, :])
                else:
                    v.tensor_tensor(r[:, :, 1, :], end_of(1), b[:, :, 1, :], ALU.subtract)
                    v.tensor_copy(r[:, :, 2, :], b[:, :, 2, :])
                    v.tensor_tensor(r[:, :, 3, :], b[:, :, 3, :], end_of(2), ALU.add)
                    link(v.tensor_tensor(r[:, :, 0, :], end_of(0), b[:, :, 0, :], ALU.subtract))
                    ins = v.tensor_tensor(r[:, :, 0, :], r[:, :, 0, :], end_of(1), ALU.add)
                ins.then_inc(sem["r_diff"], 1)

            def decayed(n):
                s = LEVELS[n]
                r1, r2 = halves(R[:, n % 2], s)
                k1, _ = halves(kT, s)
                _, q2 = halves(qT, s)
                dve.wait_ge(sem["r_exp"], n + 1)
                v.tensor_tensor(r1, r1, k1, ALU.mult)
                v.tensor_tensor(r2, r2, q2, ALU.mult).then_inc(sem["r_ready"], 1)

            def take_scores(n):
                s = LEVELS[n]
                mask = masks[:, n, :].bitcast(I32)
                for t in range(NT):
                    job = f"lv{s}_h{t}"
                    wait_full(dve, job)
                    taken(v.copy_predicated(S[:, 0:HEADS, t, :], mask.unsqueeze(1).broadcast_to([P, HEADS, P]), tiles(job, P)), job)
                for half in range(2):
                    job = f"lv{s}_g{half}"
                    wait_full(dve, job)
                    src = bank_of(job)[:, :].rearrange("p (h t i) -> p h t i", h=2, t=NT)
                    taken(v.copy_predicated(S_gla(half)[:, :, 0:NT, :],
                                            mask.unsqueeze(1).unsqueeze(1).broadcast_to([P, 2, NT, P]), src), job)

            def gate(name, g):
                for t in range(NT):
                    job = f"{name}{t}"
                    dve.wait_ge(sem["gate_sigmoid"], 2 * g + t + 1)
                    dst = gates[:, t, g * 512:(g + 1) * 512]
                    taken(v.tensor_tensor(dst, bank_of(job)[:, :], tmp[:, t, :], ALU.mult), job)
                    wait_taken(dve, job)
                    d4 = dst.rearrange("p (h n) -> p h n", n=VD)
                    v.tensor_tensor(d4, d4, onorm[:, g * VD:(g + 1) * VD].unsqueeze(1).broadcast_to([P, HEADS, VD]),
                                    ALU.mult).then_inc(sem["gate_ready"], 1)

            for job in ("b0", "b1", "b2"):
                wait_taken(dve, job)
            differences(0)
            differences(1)
            for job in ("gq", "gk", "hq0", "hq1", "fT0", "fT1"):
                wait_taken(dve, job)
            decayed(0)
            decayed(1)
            dve.wait_ge(sem["s_zeroed"], 1)
            dve.wait_ge(sem["masks_ready"], len(LEVELS) - 1)
            for n in range(7):
                if n in (2, 3):
                    gate(("hg", "gg")[n - 2], n - 2)
                take_scores(n)
                if n + 2 < 8:
                    differences(n + 2)
                    decayed(n + 2)
            v.tensor_tensor(R[:, 0], qT, kT, ALU.mult).then_inc(sem["r_ready"], 1)

            wait_taken(dve, "diag")
            for t in range(NT):
                for g, group in enumerate("hg"):
                    job = f"o{t}{group}"
                    wait_full(dve, job)
                    for h in range(HEADS):
                        hh = g * HEADS + h
                        ins = v.scalar_tensor_tensor(o_tok[:, t, hh * VD:(hh + 1) * VD], v_tok[:, t, hh * VD:(hh + 1) * VD],
                                                     dots[:, t, hh:hh + 1], bank_of(job)[:, h * VD:(h + 1) * VD], ALU.mult, ALU.add)
                    taken(ins, job)
                    wait_taken(dve, job)
                ot = o_tok[:, t, :]
                o8 = ot.rearrange("p (h n) -> p h n", n=VD)
                link(v.tensor_tensor(xn[:, t, :], ot, ot, ALU.mult))
                link(v.tensor_reduce(hsq[:, t, :], xn[:, t, :].rearrange("p (h n) -> p h n", n=VD), AX.X, ALU.add))
                inv_rms(hrms[:, t, :], hsq[:, t, :], VD)
                link(v.tensor_tensor(o8, o8, hrms[:, t, :].unsqueeze(2).broadcast_to([P, 2 * HEADS, VD]), ALU.mult))
                v.tensor_tensor(ot, ot, gates[:, t, :], ALU.mult).then_inc(sem["y_ready"], 1)

            def add_rows(prefix):
                for h in range(2):
                    for t in range(NT):
                        job = f"{prefix}{h}{t}"
                        wait_full(dve, job)
                        dst = x_res[:, t, h * 512:(h + 1) * 512]
                        taken(v.tensor_tensor(dst, dst, bank_of(job)[:, :], ALU.add), job)

            add_rows("out")
            normalise(x_res, 4, sem["x1_squared"], sem["x1_normed"])
            weigh("aT", aT, w_xa)
            for h in range(2):
                for t in range(NT):
                    wait_full(dve, f"sc{t}{h}")
                    v.tensor_reduce(nmax[:, t, 2 * h:2 * h + 2], tiles(f"sc{t}{h}", T), AX.X, ALU.max,
                                    negate=True).then_inc(sem["neg_max"], 1)
            for h in range(2):
                for t in range(NT):
                    wait_taken(dve, f"sc{t}{h}")
                    r = psums[:, t, 2 * h:2 * h + 2]
                    link(v.reciprocal(r, r))
                    p2 = probs[:, t, 2 * h:2 * h + 2, :]
                    v.tensor_tensor(p2, p2, r.unsqueeze(2).broadcast_to([P, 2, T]), ALU.mult).then_inc(sem["p_ready"], 1)
            add_rows("xo")
            dve.wait_ge(sem["moe_row_in"], 16)
            dve.wait_ge(sem["x2_squared"], NT)
            inv_rms(rstd[:, 6:8], ssq[:, 6:8], D)
            for t in range(NT):
                v.scalar_tensor_tensor(h2[:, t, :], x_res[:, t, :], rstd[:, 6 + t:7 + t], norm_row, ALU.mult,
                                       ALU.mult).then_inc(sem["h2_ready"], 1)
            dve.wait_ge(sem["router_in"], 32)
            wait_full(dve, "router")
            taken(v.tensor_tensor(logits, bank_of("router")[:, 0:NT * E].rearrange("p (t e) -> p t e", e=E),
                                  b_router.unsqueeze(1).broadcast_to([P, NT, E]), ALU.add), "router")
            wait_taken(dve, "router")
            for t in range(NT):
                link(v.max(top8[:, t, :], logits[:, t, :]))
            v.tensor_scalar(ngmax, top8[:, :, 0], -1.0, None, ALU.mult).then_inc(sem["gate_max"], 1)
            for t in range(NT):
                link(v.max_index(idx8[:, t * 8:(t + 1) * 8], top8[:, t, :], logits[:, t, :]))
            link(v.tensor_copy(idxf, idx8[:, :].rearrange("p (t e) -> p t e", t=NT)))
            for r in range(TOPK):
                for t in range(NT):
                    if r == 0:
                        ins = v.tensor_scalar(chosen[:, t, :], iota[:, 0:E], idxf[:, t, r:r + 1], None, ALU.is_equal)
                    else:
                        ins = v.scalar_tensor_tensor(chosen[:, t, :], iota[:, 0:E], idxf[:, t, r:r + 1], chosen[:, t, :],
                                                     ALU.is_equal, ALU.add)
                    if (r, t) != (TOPK - 1, NT - 1):
                        link(ins)
            ins.then_inc(sem["chosen_ready"], 1)
            dve.wait_ge(sem["chosen_ready"], 1)
            v.memset(combT, 0.0)
            v.memset(yb, 0.0).then_inc(sem["yb_ready"], 1)
            dve.wait_ge(sem["gate_exps"], NT)
            link(v.tensor_tensor(gate_tok, gate_ex, chosen, ALU.mult))
            link(v.tensor_reduce(gsum, gate_tok, AX.X, ALU.add))
            link(v.reciprocal(gsum, gsum))
            v.tensor_tensor(gate_tok, gate_tok, gsum.unsqueeze(2).broadcast_to([P, NT, E]), ALU.mult).then_inc(sem["gates_ready"], 1)
            wait_full(dve, "count")
            count = bank_of("count")[0:E, 0:1]
            link(v.tensor_scalar(nb_col, count, float(ROWS), 1.0, ALU.is_gt, ALU.add))
            for m in range(2, MAXB):
                ins = v.scalar_tensor_tensor(nb_col, count, float(m * ROWS), nb_col, ALU.is_gt, ALU.add)
                if m < MAXB - 1:
                    link(ins)
            taken(ins, "count")
            wait_full(dve, "rank")
            ins = v.scalar_tensor_tensor(rank_m, bank_of("rank")[:, 0:NT * E].rearrange("p (t e) -> p t e", e=E), 1.0, chosen,
                                         ALU.add, ALU.mult)
            taken(ins, "rank")
            wait_taken(dve, "rank")
            link(v.tensor_scalar(rank_m, rank_m, -1.0, None, ALU.add))
            wait_full(dve, "table")
            rows = bank_of("table")[0:1, 0:2 * E]
            link(v.tensor_copy(table_f[0:1, 0:2 * E], rows))
            v.tensor_copy(table[0:1, 0:2 * E], table_f[0:1, 0:2 * E])
            link(v.tensor_scalar(table_f[0:1, 2 * E:3 * E], table_f[0:1, E:2 * E], float(CHUNKS), -float(CHUNKS), ALU.mult, ALU.add))
            v.tensor_scalar(table[0:1, 2 * E:3 * E], table_f[0:1, 2 * E:3 * E], 0.0, None, ALU.max)
            taken(v.tensor_tensor(table[0:1, 3 * E:3 * E + 1], table_f[0:1, E - 1:E], table_f[0:1, 2 * E - 1:2 * E], ALU.add), "table")
            wait_taken(dve, "table")

            with dve.Fori(0, E) as e:
                blocks = dve.value_load(table[0:1, bass.ds(e, 1)], min_val=1, max_val=MAXB)
                first = dve.value_load(table[0:1, bass.ds(e + E, 1)], min_val=0, max_val=MAXB * E)
                with dve.Fori(0, blocks) as c:
                    w1 = dve.snap(first + c + 1)
                    rows = iota[:, bass.ds(c * ROWS, ROWS)]
                    v.tensor_copy(one_hot, ident[:, bass.ds(e, 1)].broadcast_to([P, ROWS]))
                    for t in range(NT):
                        ins = v.tensor_scalar(sel[:, t, :], rows, rank_m[:, t, bass.ds(e, 1)], None, ALU.is_equal)
                    ins.then_inc(sem["sel_ready"], 1)
                    dve.wait_ge(sem["gate_done"], w1)
                    v.tensor_scalar(g_t, bank_g[:, :], LIMIT, None, ALU.min).then_inc(sem["g_clamped"], 1)
                    dve.wait_ge(sem["chunk_used"], dve.snap(CHUNKS * w1 - (CHUNKS - GU_CHUNKS)))
                    v.tensor_scalar(u_t, bank_u[:, :], LIMIT, -LIMIT, ALU.min, ALU.max).then_inc(sem["u_clamped"], 1)
                    for t in range(NT):
                        for half in range(2):
                            ins = v.tensor_scalar(selg[:, t, half * ROWS:(half + 1) * ROWS], rows, rank_m[:, t, bass.ds(e, 1)],
                                                  gate_tok[:, t, bass.ds(e, 1)], ALU.is_equal, ALU.mult)
                    ins.then_inc(sem["selg_ready"], 1)
                    dve.wait_ge(sem["u_clamped"], w1)
                    v.scalar_tensor_tensor(u_t, u_t, 1.0, g_t, ALU.add, ALU.mult).then_inc(sem["up_gated"], 1)
                    dve.wait_ge(sem["up_gated"], w1)
                    dve.wait_ge(sem["sig_ready"], w1)
                    v.tensor_tensor(act_t, u_t, sg_t, ALU.mult).then_inc(sem["act_ready"], 1)
            dve.wait_ge(sem["scattered"], 1)
            for t in range(NT):
                for h in range(2):
                    dst = x_res[:, t, h * 512:(h + 1) * 512]
                    v.tensor_tensor(dst, dst, bank_y[t][h][:, :], ALU.add).then_inc(sem["out_summed"], 1)
            dve.wait_ge(sem["final_row_in"], 16)
            dve.wait_ge(sem["out_squared"], NT)
            inv_rms(rstd[:, 0:NT], ssq[:, 0:NT], D)
            for t in range(NT):
                v.scalar_tensor_tensor(xn[:, t, :], x_res[:, t, :], rstd[:, t:t + 1], norm_row, ALU.mult,
                                       ALU.mult).then_inc(sem["out_ready"], 1)


_INS = ["x", "mem", "norm_mix_w", "w_in", "hg_lb_logits", "hg_onorm_w", "gla_w_gk2", "gla_b_gk", "gla_onorm_w", "w_out",
        "norm_xa_w", "norm_mem_w", "w_xq", "w_xkv", "w_xo", "norm_moe_w", "w_router", "b_router", "w_gate_up",
        "b_gate_up", "w_down", "b_down", "norm_final_w"]


def kernel(**inputs):
    import concourse.bacc as bacc
    from concourse.bass_utils import run_bass_kernel_spmd

    nc = bacc.Bacc("TRN2", target_bir_lowering=False, num_devices=1)
    arrays, aps = {}, {}
    for name in _INS:
        a = np.ascontiguousarray(inputs[name])
        arrays[f"in_{name}"] = a
        aps[name] = nc.dram_tensor(f"in_{name}", a.shape, mybir.dt.from_np(a.dtype), kind="ExternalInput").ap()
    out = nc.dram_tensor("out_0", (1, T, D), F32, kind="ExternalOutput").ap()
    build(nc, aps, out)
    result = run_bass_kernel_spmd(nc, [arrays], core_ids=[0])
    return result.results[0]["out_0"]
```

```python
from contextlib import ExitStack

import numpy as np

import concourse.bass as bass
from concourse import mybir

F32 = mybir.dt.float32
BF16 = mybir.dt.bfloat16
I32 = mybir.dt.int32
U32 = mybir.dt.uint32
ALU = mybir.AluOpType
ACT = mybir.ActivationFunctionType
AX = mybir.AxisListType

P = 128
D = 1024
T = 256
NT = T // P
KT = D // P
EPS = 1e-6
CHUNK = 64
VD = 128
HEADS = 4
QT = 6
GKD = 64
RANK = 16
GATE_NORM = 16.0
C_HQ, C_HF, C_HI, C_HG, C_GQ, C_GV, C_GG, C_GLR = 0, 512, 1024, 1536, 2048, 2560, 3072, 3584
XH = 4
E = 32
TOPK = 4
LIMIT = 7.0
ALPHA = 1.702
ROWS = 64
MAXB = T // ROWS
CHUNKS = 12
GU_CHUNKS = KT
TWOFOLD = GU_CHUNKS + 1
WARM_UP = 14
LAST_PAIRS = 4
BIAS_PARTS = (0, 2 * E, 3 * E)
PW = 512
SLOTS = 6


PANELS = [("w_in", C_HF, "hf1"), ("w_in", C_HQ, "hq1"), ("w_in", C_GQ, "gk"), ("w_in", C_HI, "hi1"),
          ("w_in", C_GV, "gv1"), ("w_in", C_HG, "hg1"), ("w_in", C_GG, "gg1"), ("w_xkv", 0, "xk1"),
          ("w_xkv", PW, "xk3"), ("w_xkv", 2 * PW, "xv01"), ("w_out", 0, "out01"), ("w_out", PW, "out11"),
          ("w_xkv", 3 * PW, "xv11"), ("w_xq", 0, "xq1"), ("w_xq", PW, "xq3"), ("w_xo", 0, "xo01"), ("w_xo", PW, "xo11")]
LEVELS = [1, 2, 4, 8, 16, 32, 64, 128]


def four(name):
    return [f"{name}{t}{h}" for t in range(2) for h in range(2)]


def level_jobs(s):
    return [f"lv{s}_h{t}" for t in range(NT if s < P else 1)] + [f"lv{s}_g{half}" for half in range(2)]


JOBS = (four("xT") + ["hf0", "hf1", "glr", "z"] + four("mT") + ["hq0", "hq1", "fT0", "fT1", "b0", "b1", "b2", "gq", "gk"]
        + ["hi0", "hi1"] + level_jobs(1) + ["gv0", "gv1"] + level_jobs(2) + ["hg0", "hg1"] + level_jobs(4)
        + ["gg0", "gg1"] + level_jobs(8) + ["xk0", "xk1"] + level_jobs(16) + ["xk2"] + level_jobs(32)
        + level_jobs(64) + ["xv00", "xv01"] + level_jobs(128) + ["diag", "o0h", "o0g", "o1h", "o1g", "xv10"]
        + ["yT00", "yT01", "out00", "yT10", "yT11", "out10", "out01", "out11", "xk3"] + four("aT") + ["xq0", "xq1", "xq2", "xq3"]
        + ["sc00", "sc10", "sc01", "sc11", "xv11", "pT0", "pT1", "pT2", "pT3", "pv0", "pv1", "pv2", "pv3"]
        + ["xo00", "xo10", "xo01", "xo11", "eT00", "eT01", "router0", "eT10", "eT11", "router1", "rank", "count", "gT", "table"])

SEMS = """w_mix_in mem_in vec_in lb_in glr_in gk_bias_in router_in moe_row_in final_row_in down_bias_in gu_bias_in
 consts_ready ident_ready masks_ready s_zeroed x_squared x_diag mem_squared mem_diag lb_diff lb_sigmoid f_ready lnf_ready
 z_abs z_exp z_ln g_ready hq_sigmoid r_diff r_exp r_ready gate_sigmoid gate_ready y_ready x1_squared x1_diag
 neg_max p_ready x2_squared x2_diag gu_bias_zeroed gu_part_ready gu_rest_ready
 h2_ready gate_max gate_exps chosen_ready gates_ready up_gated part_ready rest_ready
 dve_step pool_step sel_ready xb_psum xb_ready comb_psum comb_ready gate_done
 g_clamped u_clamped sig_ready act_ready selg_ready chunk_used actT_psum actT_ready yb_ready
 scattered seeded out_squared out_ready stored""".split()


def build(nc, A, out):
    ctx = ExitStack()
    with ctx:
        ctx.enter_context(nc.allow_non_contiguous_dma("small vectors are laid out by feature"))

        def sb(name, cols, dt=F32, rows=P):
            return ctx.enter_context(nc.sbuf_tensor(name, [rows, cols], dt))

        sem = {n: ctx.enter_context(nc.semaphore(n)) for n in SEMS}
        bank_full = [ctx.enter_context(nc.semaphore(f"bank_full{b}")) for b in range(8)]
        bank_taken = [ctx.enter_context(nc.semaphore(f"bank_taken{b}")) for b in range(8)]
        x_in = [ctx.enter_context(nc.semaphore(f"x_in{t}")) for t in range(NT)]
        panel_in = [ctx.enter_context(nc.semaphore(f"panel_in{s}")) for s in range(SLOTS)]
        odd_in = [ctx.enter_context(nc.semaphore(f"odd_in{k}")) for k in range(TWOFOLD)]
        chunk_in = [ctx.enter_context(nc.semaphore(f"chunk_in{k}")) for k in range(CHUNKS)]
        banks = [ctx.enter_context(nc.psum_tensor(f"bank{b}", [P, 512], F32)) for b in range(8)]

        ring = sb("ring", CHUNKS * 2048)
        x_res_t = sb("x_res", NT * D)
        region1 = sb("region1", KT * T)
        region2 = sb("region2", KT * T)
        region3_tmp = sb("region3_tmp", KT * T + 1024)
        region3, tmp_t = region3_tmp[:, 0:KT * T], region3_tmp[:, KT * T:]
        region5 = sb("region5", NT * D)
        region6 = sb("region6", NT * D)
        region7 = sb("region7", 3 * QT * T)
        region10 = sb("region10", NT * D)
        r_t = sb("r_levels", 2 * QT * T)
        s_rows = sb("s_rows", 2 * HEADS * 3 * P + 1024)
        s_t, row_t = s_rows[:, 0:2 * HEADS * 3 * P], s_rows[:, 2 * HEADS * 3 * P:]
        ident = sb("ident", P)
        tri = sb("tri", P)
        strict = sb("strict", P)
        ones = sb("ones", P)
        ident3 = sb("ident3", E)
        iota = sb("iota", T)
        onorm = sb("onorm", 2 * VD)
        cols = sb("norm_cols", 4 * KT)
        stat = sb("stat", 96)
        idx8 = sb("idx8", NT * 8, U32)
        table = sb("table", 3 * E + 1, I32, rows=1)

        def fm(t, off=0):
            return t[:, off:off + KT * T].rearrange("p (k t) -> p k t", t=T)

        def tm(t, off=0, n=D):
            return t[:, off:off + NT * n].rearrange("p (t n) -> p t n", n=n)

        x_res = tm(x_res_t)
        hT, yT, aT, oT = fm(region1), fm(region1), fm(region1), fm(region1)
        memT, h2T = fm(region2), fm(region2)
        f_tok = tm(region3, 0, 512)
        zb = tm(region3, 1024, 256)
        ez = tm(region3, 1536, 256)
        xkT = fm(region3)
        b_gu = region3[:, 0:D].bitcast(BF16)
        mem_raw, v_tok = tm(region5), tm(region5)
        probs = region5[:, :].rearrange("p (t h m) -> p t h m", t=NT, h=XH)
        lb2 = region6[:, 0:1024].rearrange("p (a n) -> p a n", a=2)
        gates = tm(region6)
        probsT = region6[:, :].rearrange("p (h m t) -> p h m t", h=XH, m=2)
        qT = region7[:, 0:1536].rearrange("p (k t) -> p k t", t=T)
        kT = region7[:, 1536:3072].rearrange("p (k t) -> p k t", t=T)
        bT = region7[:, 3072:4608].rearrange("p (k t) -> p k t", t=T)
        w_glr = region7[:, 3072:3200].rearrange("p (k n) -> p k n", n=RANK)
        gk2 = region7[0:RANK, 3200:3456]
        glrT = region7[0:RANK, 3456:3712]
        sel = region7[:, 0:NT * ROWS // 2].bitcast(BF16).rearrange("p (t r) -> p t r", t=NT)
        one_hot = region7[:, 64:64 + ROWS // 2].bitcast(BF16)
        selg = region7[:, 128:384].rearrange("p (t r) -> p t r", t=NT)
        combT = region7[:, 384:640]
        xbT, actT = (region7[:, c:c + KT * ROWS].rearrange("p (k r) -> p k r", r=ROWS) for c in (640, 1152))
        act_t, g_t, u_t, sg_t, yb = (region7[:, c:c + 512] for c in range(1664, 4224, 512))
        w_router = region7[:, 1024:1280].rearrange("p (k n) -> p k n", n=E)
        b_router = region7[:, 1280:1280 + E]
        xn, h2 = tm(region10), tm(region10)
        squares = r_t[:, 2 * D:3 * D]
        R = r_t[:, :].rearrange("p (a k t) -> p a k t", a=2, t=T)
        qxT = fm(r_t)
        b_gu_raw = r_t[:, 0:2 * D]
        h2_parts = r_t[:, :].bitcast(BF16).rearrange("p (i t n) -> p i t n", i=3, t=NT)
        o_tok = r_t[:, 0:NT * D].rearrange("p (t n) -> p t n", n=D)
        S = s_t[:, :].rearrange("p (h a i) -> p h a i", h=2 * HEADS, a=3)

        def S_gla(half):
            return S[:, HEADS + half::2, :, :]

        g_tok = tm(s_t, 0, 768)
        sig_f = tm(s_t, 1536, 512)
        l_z = tm(s_t, 2560, 256)
        xv0, xv1 = tm(tmp_t, 0, 512), tm(s_t, 0, 512)
        tmp = tmp_t[:, :].rearrange("p (a n) -> p a n", a=2)
        gk_bias = tmp_t[:, 0:256]
        x_diag, mem_diag = tm(tmp_t, 512, P), tm(tmp_t, 768, P)
        x1_diag, x2_diag = tm(s_t, 2048, P), tm(s_t, 2304, P)
        small = region7[:, 1664:2176]
        odd = [region5[:, :], s_rows[:, 0:2 * D], region6[:, :], region3_tmp[:, D:3 * D], region1[:, :], s_rows[:, 2 * D:4 * D],
               region2[:, :], x_res_t[:, :], region10[:, :]]
        masks = row_t[:, 0:(len(LEVELS) - 1) * P].rearrange("p (l i) -> p l i", i=P)
        norm_row = row_t[:, :]
        w_mix, w_xa, w_mem, w_moe = (cols[:, i * KT:(i + 1) * KT] for i in range(4))
        rstd = stat[:, 0:8]
        ssq = stat[:, 8:16]
        hsq = stat[:, 16:32].rearrange("p (t h) -> p t h", t=NT)
        hrms = stat[:, 64:80].rearrange("p (t h) -> p t h", t=NT)
        newton = stat[:, 80:96].rearrange("p (a n) -> p a n", a=2)
        dots = stat[:, 32:48].rearrange("p (t h) -> p t h", t=NT)
        nmax = stat[:, 48:56].rearrange("p (t h) -> p t h", t=NT)
        psums = stat[:, 56:64].rearrange("p (t h) -> p t h", t=NT)
        logits, chosen, gate_ex = (small[:, c:c + NT * E].rearrange("p (t e) -> p t e", t=NT) for c in range(0, 192, 64))
        gate_tok, rank_m = (region7[:, c:c + NT * E].rearrange("p (t e) -> p t e", t=NT) for c in (4224, 4288))
        top8, idxf = (small[:, c:c + NT * 8].rearrange("p (t e) -> p t e", t=NT) for c in (320, 336))
        gsum, ngmax, nb_col = small[:, 352:354], small[:, 354:356], small[0:E, 356:357]
        table_f = small[0:1, 360:360 + 3 * E]

        def panel(n):
            s = n % SLOTS
            return ring[:, s * 4096:(s + 1) * 4096].rearrange("p (k n) -> p k n", n=PW)

        def chunk(k):
            return ring[:, k * 2048:(k + 1) * 2048]

        def bank_of(job):
            return banks[JOBS.index(job) % 8]

        def wait_full(eng, job):
            n = JOBS.index(job)
            eng.wait_ge(bank_full[n % 8], n // 8 + 1)

        def wait_taken(eng, job):
            n = JOBS.index(job)
            eng.wait_ge(bank_taken[n % 8], n // 8 + 1)

        def taken(ins, job):
            ins.then_inc(bank_taken[JOBS.index(job) % 8], 1)

        bank_y = [[bank_of("eT10"), bank_of("router0")], [bank_of("eT11"), bank_of("router1")]]
        bank_a, bank_g, bank_u, bank_d = (bank_of(job) for job in ("rank", "count", "table", "gT"))
        block = ctx.enter_context(nc.Block())

        def by_feature(v):
            return v.rearrange("(k p) -> p k", p=P)

        @block.sync
        def _(sp):
            for t in range(NT):
                sp.dma_start(x_res[:, t, :], A["x"][0, t * P:(t + 1) * P, :]).then_inc(x_in[t], 16)
            sp.dma_start(w_mix, by_feature(A["norm_mix_w"][0])).then_inc(sem["w_mix_in"], 16)
            weight = {"w_in": A["w_in"], "w_xkv": A["w_xkv"], "w_out": A["w_out"], "w_xq": A["w_xq"], "w_xo": A["w_xo"]}
            for n, (name, c0, _) in enumerate(PANELS):
                if n >= SLOTS:
                    wait_full(sp, PANELS[n - SLOTS][2])
                src = weight[name][0, :, c0:c0 + PW].rearrange("(k p) n -> p k n", p=P)
                sp.dma_start(panel(n), src).then_inc(panel_in[n % SLOTS], 16)
                if n == 0:
                    sp.dma_start(lb2, A["hg_lb_logits"].rearrange("(o a) n -> o a n", o=1).broadcast_to([P, 2, 512])).then_inc(sem["lb_in"], 16)
                    sp.dma_start(w_glr, A["w_in"][0, :, C_GLR:C_GLR + RANK].rearrange("(k p) n -> p k n", p=P)).then_inc(sem["glr_in"], 16)
                    sp.dma_start(gk2, A["gla_w_gk2"][0]).then_inc(sem["glr_in"], 16)
                    sp.dma_start(gk_bias, A["gla_b_gk"].broadcast_to([P, 256])).then_inc(sem["gk_bias_in"], 16)
                    sp.dma_start(mem_raw, A["mem"][0].rearrange("(t p) n -> p t n", p=P)).then_inc(sem["mem_in"], 16)
                    sp.dma_start(w_mem, by_feature(A["norm_mem_w"][0])).then_inc(sem["vec_in"], 16)
                    sp.dma_start(w_moe, by_feature(A["norm_moe_w"][0])).then_inc(sem["vec_in"], 16)
                    sp.dma_start(w_xa, by_feature(A["norm_xa_w"][0])).then_inc(sem["vec_in"], 16)
                    sp.dma_start(onorm[:, 0:VD], A["hg_onorm_w"].broadcast_to([P, VD])).then_inc(sem["vec_in"], 16)
                    sp.dma_start(onorm[:, VD:2 * VD], A["gla_onorm_w"].broadcast_to([P, VD])).then_inc(sem["vec_in"], 16)

            def load_chunk(e, k, odd_e=False):
                dst, signal = (odd[k], odd_in[k]) if odd_e and k < TWOFOLD else (chunk(k), chunk_in[k])
                if k < GU_CHUNKS:
                    src = A["w_gate_up"][0, e, k * P:(k + 1) * P, :]
                else:
                    j = k - GU_CHUNKS
                    src = A["w_down"][0, e, 2 * j * P:(2 * j + 2) * P, :].rearrange("(a p) n -> p a n", p=P)
                    dst = dst.rearrange("p (a n) -> p a n", a=2)
                sp.dma_start(dst, src).then_inc(signal, 16)

            slots = {PANELS[n][2]: n % SLOTS for n in range(len(PANELS) - SLOTS, len(PANELS))}
            places = {"pT3": [0], "pv3": [1, 2, 3], "xo11": [4], "eT11": [5], "router1": [6]}
            for job in JOBS:
                if job in slots or job in places:
                    wait_full(sp, job)
                if job in slots:
                    load_chunk(0, 2 * slots[job])
                    load_chunk(0, 2 * slots[job] + 1)
                if job == "eT11":
                    sp.wait_ge(sem["h2_ready"], NT)
                for k in places.get(job, []):
                    load_chunk(1, k, True)
            sp.wait_ge(sem["seeded"], 2 * NT)
            load_chunk(1, 7, True)
            sp.wait_ge(sem["part_ready"], 3 * NT)
            load_chunk(1, 8, True)
            wait_taken(sp, "table")

            def refill(e, chunks, odd_e, ahead):
                used = sp.value_load(table[0:1, bass.ds(e + 2 * E + 1, 1)], min_val=0, max_val=CHUNKS * MAXB * E)
                for k in chunks:
                    sp.wait_ge(sem["chunk_used"], used + (k + 1))
                    load_chunk(e + ahead, k, odd_e)

            twofold, single = range(TWOFOLD), range(TWOFOLD, CHUNKS)
            with sp.Fori(0, E // 2 - 1 - LAST_PAIRS) as i:
                for parity in range(2):
                    e = sp.snap(2 * i + parity)
                    refill(e, twofold, parity == 1, 2)
                    refill(e, single, False, 1)
            with sp.Fori(E // 2 - 1 - LAST_PAIRS, E // 2 - 1) as i:
                for parity in range(2):
                    e = sp.snap(2 * i + parity)
                    refill(e, single, False, 1)
                    refill(e, twofold, parity == 1, 2)
            refill(E - 2, single, False, 1)
            total = sp.value_load(table[0:1, 3 * E:3 * E + 1], min_val=E, max_val=MAXB * E)
            sp.wait_ge(sem["chunk_used"], sp.snap(total * CHUNKS))
            sp.dma_start(norm_row, A["norm_final_w"].rearrange("(o n) -> o n", o=1).broadcast_to([P, D])).then_inc(sem["final_row_in"], 16)
            for t in range(NT):
                for h in range(2):
                    sp.wait_ge(sem["out_ready"], 2 * t + h + 1)
                    sp.dma_start(out[0, t * P:(t + 1) * P, h * 512:(h + 1) * 512],
                                 xn[:, t, h * 512:(h + 1) * 512]).then_inc(sem["stored"], 16)
            sp.wait_ge(sem["stored"], 16 * 2 * NT)

        @block.gpsimd
        def _(pool):
            steps = [0]

            def link(ins):
                steps[0] += 1
                ins.then_inc(sem["pool_step"], 1)
                pool.wait_ge(sem["pool_step"], steps[0])

            link(pool.memset(ident[:, :], 0.0))
            pool.affine_select(out=ident[:, :], in_=ident[:, :], compare_op=ALU.not_equal, fill=1.0, base=0,
                               pattern=[[-1, P]], channel_multiplier=1).then_inc(sem["ident_ready"], 1)
            link(pool.memset(ones[:, :], 1.0))
            link(pool.affine_select(out=tri[:, :], in_=ones[:, :], compare_op=ALU.is_ge, fill=0.0, base=0,
                                    pattern=[[1, P]], channel_multiplier=-1))
            link(pool.memset(tri[0:CHUNK, CHUNK:P], 0.0))
            link(pool.affine_select(out=strict[:, :], in_=ones[:, :], compare_op=ALU.is_gt, fill=0.0, base=0,
                                    pattern=[[1, P]], channel_multiplier=-1))
            link(pool.memset(ident3[:, :], 0.0))
            for first in BIAS_PARTS:
                link(pool.affine_select(out=ident3[:, :], in_=ident3[:, :], compare_op=ALU.not_equal, fill=1.0, base=-first,
                                        pattern=[[-1, E]], channel_multiplier=1))
            pool.iota(iota[:, :], pattern=[[1, T]], base=0, channel_multiplier=0,
                      allow_small_or_imprecise_dtypes=True).then_inc(sem["consts_ready"], 1)
            for n, s in enumerate(LEVELS[:-1]):
                m = masks[:, n, :].rearrange("p (b a r) -> p b a r", a=2, r=s)
                link(pool.memset(masks[:, n, :], 0.0))
                link(pool.memset(m[:, :, 1, :], 1.0))
                link(pool.affine_select(out=m[:, :, 1, :], in_=m[:, :, 1, :], compare_op=ALU.is_ge, fill=0.0, base=0,
                                        pattern=[[-2 * s, P // (2 * s)], [0, s]], channel_multiplier=1))
                pool.affine_select(out=m[:, :, 1, :], in_=m[:, :, 1, :], compare_op=ALU.is_gt, fill=0.0, base=s,
                                   pattern=[[2 * s, P // (2 * s)], [0, s]], channel_multiplier=-1).then_inc(sem["masks_ready"], 1)
            for job in ("b0", "b1", "b2"):
                wait_full(pool, job)
            pool.memset(s_t[:, :], 0.0).then_inc(sem["s_zeroed"], 1)
            wait_full(pool, "diag")
            pool.dma_start(w_router, A["w_router"][0].rearrange("(k p) n -> p k n", p=P)).then_inc(sem["router_in"], 16)
            pool.dma_start(b_router, A["b_router"].broadcast_to([P, E])).then_inc(sem["router_in"], 16)
            for job in level_jobs(64):
                wait_taken(pool, job)
            pool.dma_start(norm_row, A["norm_moe_w"].broadcast_to([P, D])).then_inc(sem["moe_row_in"], 16)
            pool.memset(yb, 0.0).then_inc(sem["yb_ready"], 1)
            pool.wait_ge(sem["yb_ready"], 1)
            for half in range(2):
                pool.dma_start(yb[half * ROWS:half * ROWS + E, :],
                               A["b_down"][0, :, half * 512:(half + 1) * 512]).then_inc(sem["down_bias_in"], 16)
            wait_full(pool, "sc11")
            for first in BIAS_PARTS:
                pool.dma_start(b_gu_raw[first:first + E, :], A["b_gate_up"][0]).then_inc(sem["gu_bias_in"], 16)
            pool.memset(b_gu[E:2 * E, :], 0.0).then_inc(sem["gu_bias_zeroed"], 1)
            pool.wait_ge(sem["gu_bias_zeroed"], 1)
            for i in range(2):
                for t in range(NT):
                    pool.wait_ge(sem["part_ready"], i * NT + t + 1)
                    pool.tensor_tensor(h2[:, t, :], h2[:, t, :], h2_parts[:, i, t], ALU.subtract).then_inc(sem["rest_ready"], 1)
        @block.tensor
        def _(pe):
            begun, done = [0], [0]

            def begin(job):
                n = begun[0]
                begun[0] += 1
                assert JOBS[n] == job, (JOBS[n], job)
                if n >= 8:
                    wait_taken(pe, JOBS[n - 8])
                return banks[n % 8]

            def end(ins):
                ins.then_inc(bank_full[done[0] % 8], 1)
                done[0] += 1

            def arrived(first_job_weight, c0):
                n = [p[:2] for p in PANELS].index((first_job_weight, c0))
                pe.wait_ge(panel_in[n % SLOTS], 16 * (n // SLOTS + 1))
                return panel(n)

            def transposes(prefix, t, src, rhs):
                for h in range(2):
                    bk = begin(f"{prefix}{t}{h}")
                    for i in range(4):
                        k = 4 * h + i
                        last = pe.matmul(bk[:, i * P:(i + 1) * P], src[:, t, k * P:(k + 1) * P], rhs, start=True, stop=True)
                    end(last)

            def normed_transposes(prefix, src, diag, ready):
                for t in range(NT):
                    pe.wait_ge(ready, t + 1)
                    transposes(prefix, t, src, diag[:, t, :])

            def await_rows(needs, k):
                for job in needs.get(k, []):
                    wait_taken(pe, job)

            def by_feature(job, w, m, rhs, needs={}):
                bk = begin(job)
                for i in range(2):
                    for k in range(KT):
                        if i == 0:
                            await_rows(needs, k)
                        last = pe.matmul(bk[:, i * T:(i + 1) * T], w[:, k, (m + i) * P:(m + i + 1) * P], rhs[:, k, :],
                                         start=(k == 0), stop=(k == KT - 1))
                end(last)

            def by_token(job, w, t, lhs, needs={}):
                bk = begin(job)
                for k in range(KT):
                    await_rows(needs, k)
                    last = pe.matmul(bk[:, :], lhs[:, k, t * P:(t + 1) * P], w[:, k, :], start=(k == 0), stop=(k == KT - 1))
                end(last)

            def level(n):
                pe.wait_ge(sem["r_ready"], n + 1)
                s = LEVELS[n]
                tiles = [(t, t) for t in range(NT)] if s < P else [(0, 1)]

                def scores(out_, rows, j, i):
                    return pe.matmul(out_, rows[:, j * P:(j + 1) * P], rows[:, i * P:(i + 1) * P], start=True, stop=True)

                for j, i in tiles:
                    bk = begin(f"lv{s}_h{j}")
                    for h in range(HEADS):
                        last = scores(bk[:, h * P:(h + 1) * P], R[:, n % 2, h, :], j, i)
                    end(last)
                pair_banks = [begin(f"lv{s}_g{half}") for half in range(2)]
                for h in range(2):
                    for a, (j, i) in enumerate(tiles):
                        c = (h * len(tiles) + a) * P
                        last = [scores(pair_banks[half][:, c:c + P], R[GKD * half:GKD * (half + 1), n % 2, HEADS + h, :], j, i)
                                for half in range(2)]
                for half in range(2):
                    end(last[half])

            pe.wait_ge(sem["ident_ready"], 1)
            for n in range(WARM_UP):
                pe.matmul(banks[7][:, 0:P], ident[:, :], ident[:, :], start=(n == 0), stop=(n == WARM_UP - 1))
            pe.wait_ge(sem["consts_ready"], 1)
            normed_transposes("xT", x_res, x_diag, sem["x_diag"])
            w = arrived("w_in", C_HF)
            by_token("hf0", w, 0, hT, {0: ["xT00"], 4: ["xT01"]})
            by_token("hf1", w, 1, hT, {0: ["xT10"], 4: ["xT11"]})
            pe.wait_ge(sem["glr_in"], 32)
            bk = begin("glr")
            for k in range(KT):
                last = pe.matmul(bk[0:RANK, 0:T], w_glr[:, k, :], hT[:, k, :], start=(k == 0), stop=(k == KT - 1))
            end(last)
            wait_taken(pe, "glr")
            bk = begin("z")
            for t in range(NT):
                last = pe.matmul(bk[:, t * 256:(t + 1) * 256], glrT[:, t * P:(t + 1) * P], gk2, start=True, stop=True)
            end(last)
            normed_transposes("mT", mem_raw, mem_diag, sem["mem_diag"])
            w = arrived("w_in", C_HQ)
            by_feature("hq0", w, 0, hT)
            by_feature("hq1", w, 2, hT)
            pe.wait_ge(sem["f_ready"], NT)
            for i in range(2):
                bk = begin(f"fT{i}")
                for a in range(2):
                    for t in range(NT):
                        last = pe.transpose(bk[:, a * T + t * P:a * T + (t + 1) * P],
                                            f_tok[:, t, (2 * i + a) * P:(2 * i + a + 1) * P], ident[:, :])
                end(last)
            pe.wait_ge(sem["lnf_ready"], NT)
            pe.wait_ge(sem["g_ready"], 1)
            for i in range(3):
                bk = begin(f"b{i}")
                for a in range(2):
                    for t in range(NT):
                        last = pe.matmul(bk[:, a * T + t * P:a * T + (t + 1) * P],
                                         g_tok[:, t, (2 * i + a) * P:(2 * i + a + 1) * P], tri[:, :], start=True, stop=True)
                end(last)
            w = arrived("w_in", C_GQ)
            by_feature("gq", w, 0, hT)
            by_feature("gk", w, 2, hT)
            for n, (name, c0) in enumerate((("hi", C_HI), ("gv", C_GV), ("hg", C_HG), ("gg", C_GG))):
                w = arrived("w_in", c0)
                by_token(f"{name}0", w, 0, hT)
                by_token(f"{name}1", w, 1, hT)
                level(n)
            for job in four("mT"):
                wait_taken(pe, job)
            w = arrived("w_xkv", 0)
            by_feature("xk0", w, 0, memT)
            by_feature("xk1", w, 2, memT)
            level(4)
            by_feature("xk2", arrived("w_xkv", PW), 0, memT)
            level(5)
            level(6)
            w = arrived("w_xkv", 2 * PW)
            by_token("xv00", w, 0, memT)
            by_token("xv01", w, 1, memT)
            level(7)
            pe.wait_ge(sem["r_ready"], 9)
            bk = begin("diag")
            for k in range(QT):
                for t in range(NT):
                    if k < HEADS:
                        c, n, rhs = t * 2 * HEADS + k, 1, ones[:, 0:1]
                    else:
                        c, n, rhs = t * 2 * HEADS + HEADS + 2 * (k - HEADS), 2, tri[:, CHUNK - 1::CHUNK]
                    last = pe.matmul(bk[:, c:c + n], R[:, 0, k, t * P:(t + 1) * P], rhs, start=True, stop=True)
            end(last)
            for job in level_jobs(64) + level_jobs(128) + ["hi0", "hi1", "gv0", "gv1"]:
                wait_taken(pe, job)
            for t in range(NT):
                for g, group in enumerate("hg"):
                    bk = begin(f"o{t}{group}")
                    for h in range(HEADS):
                        hh = g * HEADS + h
                        parts = [(0, 0)] if t == 0 else [(2, 0), (1, 1)]
                        for a, j in parts:
                            last = pe.matmul(bk[:, h * VD:(h + 1) * VD], S[:, hh, a, :], v_tok[:, j, hh * VD:(hh + 1) * VD],
                                             start=(j == 0), stop=(j == t))
                    end(last)
            w = arrived("w_xkv", 3 * PW)
            by_token("xv10", w, 0, memT)
            def mix(t, i):
                by_token(f"out{i}{t}", arrived("w_out", i * PW), t, yT, {0: [f"yT{t}0"], 4: [f"yT{t}1"]})

            pe.wait_ge(sem["y_ready"], 1)
            transposes("yT", 0, o_tok, ident[:, :])
            mix(0, 0)
            pe.wait_ge(sem["y_ready"], 2)
            transposes("yT", 1, o_tok, ident[:, :])
            mix(0, 1)
            mix(1, 0)
            mix(1, 1)
            by_feature("xk3", arrived("w_xkv", PW), 2, memT)
            normed_transposes("aT", x_res, x1_diag, sem["x1_diag"])
            for i in range(2):
                w = arrived("w_xq", i * PW)
                by_feature(f"xq{2 * i}", w, 0, aT, {0: ["aT00", "aT10"], 4: ["aT01", "aT11"]})
                by_feature(f"xq{2 * i + 1}", w, 2, aT)
            for h in range(2):
                for job in (f"xk{2 * h}", f"xk{2 * h + 1}", f"xq{2 * h}", f"xq{2 * h + 1}"):
                    wait_taken(pe, job)
                for t in range(NT):
                    bk = begin(f"sc{t}{h}")
                    for i in range(2):
                        for a in range(2):
                            k = 2 * (2 * h + i) + a
                            last = pe.matmul(bk[:, i * T:(i + 1) * T], qxT[:, k, t * P:(t + 1) * P], xkT[:, k, :],
                                             start=(a == 0), stop=(a == 1))
                    end(last)
            by_token("xv11", arrived("w_xkv", 3 * PW), 1, memT)
            for h in range(XH):
                pe.wait_ge(sem["p_ready"], 2 * (h // 2) + 2)
                bk = begin(f"pT{h}")
                for m in range(2):
                    for t in range(NT):
                        last = pe.transpose(bk[:, m * T + t * P:m * T + (t + 1) * P], probs[:, t, h, m * P:(m + 1) * P], ident[:, :])
                end(last)
            for job in ["xv00", "xv01", "xv10", "xv11"]:
                wait_taken(pe, job)
            for h in range(XH):
                wait_taken(pe, f"pT{h}")
                bk = begin(f"pv{h}")
                for a in range(2):
                    c = (2 * (h % 2) + a) * P
                    for m in range(2):
                        last = pe.matmul(bk[:, a * T:(a + 1) * T], (xv0, xv1)[h // 2][:, m, c:c + P], probsT[:, h, m, :],
                                         start=(m == 0), stop=(m == 1))
                end(last)
            for t in range(NT):
                for i in range(2):
                    by_token(f"xo{i}{t}", arrived("w_xo", i * PW), t, oT, {2 * h: [f"pv{h}"] for h in range(XH)})
            pe.wait_ge(sem["router_in"], 32)

            def seed(t, half):
                wait_taken(pe, (("eT10", "router0"), ("eT11", "router1"))[t][half])
                pe.matmul(bank_y[t][half][:, :], ident[:, :], x_res[:, t, half * 512:(half + 1) * 512], start=True, stop=False,
                          skip_group_check=True).then_inc(sem["seeded"], 1)

            for t in range(NT):
                pe.wait_ge(sem["x2_diag"], t + 1)
                transposes("eT", t, x_res, x2_diag[:, t, :])
                if t == 1:
                    seed(0, 0)
                bk = begin(f"router{t}")
                for k in range(KT):
                    await_rows({0: [f"eT{t}0"], 4: [f"eT{t}1"]}, k)
                    last = pe.matmul(bk[:, 0:E], h2T[:, k, t * P:(t + 1) * P], w_router[:, k, :], start=(k == 0), stop=(k == KT - 1))
                end(last)
            for t, half in ((0, 1), (1, 0), (1, 1)):
                seed(t, half)
            rank, count = begin("rank"), begin("count")
            pe.wait_ge(sem["chosen_ready"], 1)
            pe.matmul(rank[:, 0:E], strict[:, :], chosen[:, 0, :], start=True, stop=True)
            pe.matmul(rank[:, E:2 * E], ones[:, :], chosen[:, 0, :], start=True, stop=False)
            pe.matmul(count[0:E, 0:1], chosen[:, 0, :], ones[:, 0:1], start=True, stop=False)
            pe.wait_ge(sem["chosen_ready"], NT)
            end(pe.matmul(rank[:, E:2 * E], strict[:, :], chosen[:, 1, :], start=False, stop=True))
            end(pe.matmul(count[0:E, 0:1], chosen[:, 1, :], ones[:, 0:1], start=False, stop=True))
            pe.wait_ge(sem["gates_ready"], 1)
            bk = begin("gT")
            for t in range(NT):
                last = pe.transpose(bk[:, t * P:(t + 1) * P], selg[:, t, :], ident[:, :])
            end(last)
            wait_taken(pe, "count")
            bk = begin("table")
            pe.matmul(bk[0:1, 0:E], nb_col, ident[0:E, 0:E], start=True, stop=True)
            end(pe.matmul(bk[0:1, E:2 * E], nb_col, strict[0:E, 0:E], start=True, stop=True))

            for job in JOBS[-4:]:
                wait_taken(pe, job)
            pe.wait_ge(sem["part_ready"], 3 * NT)
            pe.wait_ge(sem["gu_bias_zeroed"], 1)
            pe.wait_ge(sem["gu_part_ready"], 3)
            pe.wait_ge(sem["down_bias_in"], 32)

            def pair(bk, lhs, w, start, stop):
                for half in range(2):
                    last = pe.matmul(bk[half * ROWS:(half + 1) * ROWS, :], lhs, w[:, half * 512:(half + 1) * 512],
                                     start=start, stop=stop, skip_group_check=True)
                return last

            def scatter(signal=None):
                for t in range(NT):
                    for half in range(2):
                        rows = slice(half * ROWS, (half + 1) * ROWS)
                        last = pe.matmul(bank_y[t][half][:, :], combT[rows, t * P:(t + 1) * P], yb[rows, :],
                                         start=False, stop=False, skip_group_check=True)
                    if signal is not None:
                        last.then_inc(signal, 1)

            def expert(e, places, arrivals):
                blocks = pe.value_load(table[0:1, bass.ds(e, 1)], min_val=1, max_val=MAXB)
                first = pe.value_load(table[0:1, bass.ds(e + E, 1)], min_val=0, max_val=MAXB * E)
                with pe.Fori(0, blocks) as c:
                    w1 = pe.snap(first + c + 1)
                    pe.wait_ge(sem["sel_ready"], w1)
                    for k in range(KT):
                        for i in range(3):
                            for t in range(NT):
                                last = pe.matmul(bank_a[:, k * ROWS:(k + 1) * ROWS], h2_parts[:, i, t, k * P:(k + 1) * P],
                                                 sel[:, t, :], start=(i == 0 and t == 0), stop=(i == 2 and t == NT - 1),
                                                 skip_group_check=True)
                    last.then_inc(sem["xb_psum"], 1)
                    for bk, c0 in ((bank_g, 0), (bank_u, D)):
                        pair(bk, one_hot, b_gu[:, c0:c0 + D], True, False)
                    pe.wait_ge(sem["xb_ready"], w1)
                    for k in range(GU_CHUNKS):
                        pe.wait_ge(*arrivals[k])
                        wk = places[k]
                        last = pair(bank_g, xbT[:, k, :], wk[:, 0:D], False, k == KT - 1)
                        if k == KT - 1:
                            last.then_inc(sem["gate_done"], 1)
                        pair(bank_u, xbT[:, k, :], wk[:, D:2 * D], False, k == KT - 1).then_inc(sem["chunk_used"], 1)
                    pe.wait_ge(sem["yb_ready"], w1)
                    scatter()
                    pe.wait_ge(sem["selg_ready"], w1)
                    for t in range(NT):
                        last = pe.matmul(bank_d[:, t * P:(t + 1) * P], selg[:, t, :], ident[:, :], start=True, stop=True,
                                         is_transpose=True, skip_group_check=True)
                    last.then_inc(sem["comb_psum"], 1)
                    pe.wait_ge(sem["act_ready"], w1)
                    for i in range(4):
                        last = pe.matmul(bank_a[:, i * P:(i + 1) * P], act_t[:, i * P:(i + 1) * P], ident[:, :], start=True,
                                         stop=True, is_transpose=True, skip_group_check=True)
                    last.then_inc(sem["actT_psum"], 1)
                    pe.wait_ge(sem["comb_ready"], w1)
                    pe.wait_ge(sem["actT_ready"], w1)
                    for j in range(CHUNKS - GU_CHUNKS):
                        pe.wait_ge(*arrivals[GU_CHUNKS + j])
                        for a in range(2):
                            f = 2 * j + a
                            last = pair(bank_d, actT[:, f, :], places[GU_CHUNKS + j][:, a * D:(a + 1) * D], f == 0, f == KT - 1)
                        last.then_inc(sem["chunk_used"], 1)
            ring_places = [chunk(k) for k in range(CHUNKS)]
            with pe.Fori(0, E // 2) as i:
                n_pair, n_even, n_odd = pe.snap(16 * i + 16), pe.snap(32 * i + 16), pe.snap(32 * i + 32)
                expert(pe.snap(2 * i), ring_places,
                       [(chunk_in[k], n_pair if k < TWOFOLD else n_even) for k in range(CHUNKS)])
                expert(pe.snap(2 * i + 1), odd + ring_places[TWOFOLD:],
                       [(odd_in[k], n_pair) for k in range(TWOFOLD)] + [(chunk_in[k], n_odd) for k in range(TWOFOLD, CHUNKS)])
            total = pe.value_load(table[0:1, 3 * E:3 * E + 1], min_val=E, max_val=MAXB * E)
            pe.wait_ge(sem["yb_ready"], pe.snap(total + 1))
            scatter(sem["scattered"])

        @block.scalar
        def _(act):
            def fn(out_, in_, func, **kw):
                return nc.scalar.activation(out_, in_, func, **kw)

            def rows_squared(src, i, t, signal):
                fn(squares, src[:, t, :], ACT.Square, accum_out=ssq[:, i + t:i + t + 1]).then_inc(signal, 1)
                act.wait_ge(signal, t + 1)

            def take(job, dst, src=None, **kw):
                wait_full(act, job)
                src = bank_of(job)[:, :] if src is None else src
                taken(fn(dst, src, ACT.Copy, **kw), job)

            def tiles(job, n):
                return bank_of(job)[:, :].rearrange("p (k t) -> p k t", t=n)

            for t in range(NT):
                act.wait_ge(x_in[t], 16)
                rows_squared(x_res, 0, t, sem["x_squared"])
            act.wait_ge(sem["mem_in"], 16)
            for t in range(NT):
                rows_squared(mem_raw, 2, t, sem["mem_squared"])
            act.wait_ge(sem["lb_diff"], 1)
            fn(lb2[:, 0, :], lb2[:, 0, :], ACT.Sigmoid).then_inc(sem["lb_sigmoid"], 1)
            for t in range(NT):
                wait_full(act, f"hf{t}")
                taken(fn(sig_f[:, t, :], bank_of(f"hf{t}")[:, :], ACT.Sigmoid), f"hf{t}")
            take("glr", glrT, bank_of("glr")[0:RANK, 0:T])
            act.wait_ge(sem["z_abs"], 1)
            fn(ez, ez, ACT.Exp).then_inc(sem["z_exp"], 1)
            act.wait_ge(sem["z_exp"], 1)
            fn(l_z, ez, ACT.Ln, bias=1.0).then_inc(sem["z_ln"], 1)
            for t in range(NT):
                act.wait_ge(sem["f_ready"], t + 1)
                fn(g_tok[:, t, 0:512], f_tok[:, t, :], ACT.Ln).then_inc(sem["lnf_ready"], 1)
            for i in range(2):
                wait_full(act, f"hq{i}")
                fn(tmp[:, i, :], bank_of(f"hq{i}")[:, :], ACT.Sigmoid).then_inc(sem["hq_sigmoid"], 1)
            for i in range(3):
                take(f"b{i}", bT[:, 2 * i:2 * i + 2, :], tiles(f"b{i}", T), scale=1.0 if i < 2 else 1.0 / GATE_NORM)
            take("gq", qT[:, 4:6, :], tiles("gq", T), scale=GKD ** -0.5)
            take("gk", kT[:, 4:6, :], tiles("gk", T))

            def decay(n):
                act.wait_ge(sem["r_diff"], n + 1)
                fn(R[:, n % 2], R[:, n % 2], ACT.Exp).then_inc(sem["r_exp"], 1)

            def gate_sigmoid(name, i):
                for t in range(NT):
                    if i == 0:
                        wait_taken(act, f"hq{t}")
                    else:
                        act.wait_ge(sem["gate_ready"], t + 1)
                    wait_full(act, f"{name}{t}")
                    fn(tmp[:, t, :], bank_of(f"{name}{t}")[:, :], ACT.Sigmoid).then_inc(sem["gate_sigmoid"], 1)

            decay(0)
            decay(1)
            take("hi0", v_tok[:, 0, 0:512])
            take("hi1", v_tok[:, 1, 0:512])
            decay(2)
            take("gv0", v_tok[:, 0, 512:1024])
            take("gv1", v_tok[:, 1, 512:1024])
            decay(3)
            gate_sigmoid("hg", 0)
            decay(4)
            gate_sigmoid("gg", 1)
            decay(5)
            take("xk0", xkT[:, 0:2, :], tiles("xk0", T))
            take("xk1", xkT[:, 2:4, :], tiles("xk1", T))
            decay(6)
            take("xk2", xkT[:, 4:6, :], tiles("xk2", T))
            decay(7)
            act.wait_ge(sem["gate_ready"], 4)
            for t in range(NT):
                take(f"xv0{t}", xv0[:, t, :])
            take("lv128_h0", S[:, 0:HEADS, 2, :], tiles("lv128_h0", P))
            for half in range(2):
                take(f"lv128_g{half}", S_gla(half)[:, :, 2, :], tiles(f"lv128_g{half}", P)[:, 0:2, :])
            take("diag", stat[:, 32:48], bank_of("diag")[:, 0:16])
            take("xv10", xv1[:, 0, :])
            for t in range(NT):
                for h in range(2):
                    take(f"yT{t}{h}", yT[:, 4 * h:4 * h + 4, t * P:(t + 1) * P], tiles(f"yT{t}{h}", P))
            for t in range(NT):
                for h in range(2):
                    wait_taken(act, f"out{h}{t}")
                rows_squared(x_res, 4, t, sem["x1_squared"])
            take("xk3", xkT[:, 6:8, :], tiles("xk3", T))
            for j in range(4):
                take(f"xq{j}", qxT[:, 2 * j:2 * j + 2, :], tiles(f"xq{j}", T), scale=(D // XH) ** -0.5)
            for h in range(2):
                for t in range(NT):
                    job = f"sc{t}{h}"
                    act.wait_ge(sem["neg_max"], 2 * h + t + 1)
                    for i in range(2):
                        a = 2 * h + i
                        ins = fn(probs[:, t, a, :], bank_of(job)[:, i * T:(i + 1) * T], ACT.Exp,
                                 bias=nmax[:, t, a:a + 1], accum_out=psums[:, t, a:a + 1])
                    taken(ins, job)
            take("xv11", xv1[:, 1, :])
            for h in range(XH):
                take(f"pT{h}", probsT[:, h], tiles(f"pT{h}", T))
            for h in range(XH):
                take(f"pv{h}", oT[:, 2 * h:2 * h + 2, :], tiles(f"pv{h}", T))
            act.wait_ge(sem["gu_bias_in"], 16 * 3)
            for i, first in enumerate(BIAS_PARTS):
                if i:
                    act.wait_ge(sem["gu_rest_ready"], i)
                if i == 0:
                    fn(b_gu[0:E, :], b_gu_raw[0:E, :], ACT.Copy)
                    fn(b_gu[2 * E:P, :], b_gu_raw[2 * E:P, :], ACT.Copy).then_inc(sem["gu_part_ready"], 1)
                else:
                    fn(b_gu[first:P, :], b_gu_raw[first:P, :], ACT.Copy).then_inc(sem["gu_part_ready"], 1)
            for t in range(NT):
                for h in range(2):
                    wait_taken(act, f"xo{h}{t}")
                rows_squared(x_res, 6, t, sem["x2_squared"])

            def cut(i, t):
                if i == 0:
                    act.wait_ge(sem["h2_ready"], t + 1)
                else:
                    act.wait_ge(sem["rest_ready"], (i - 1) * NT + t + 1)
                fn(h2_parts[:, i, t], h2[:, t, :], ACT.Copy).then_inc(sem["part_ready"], 1)

            def gate_exps(t):
                act.wait_ge(sem["gate_max"], t + 1)
                fn(gate_ex[:, t, :], logits[:, t, :], ACT.Exp, bias=ngmax[:, t:t + 1]).then_inc(sem["gate_exps"], 1)

            cut(0, 0)
            cut(0, 1)
            cut(1, 0)
            cut(1, 1)
            gate_exps(0)
            gate_exps(1)
            cut(2, 0)
            cut(2, 1)
            take("gT", combT, bank_of("gT")[:, 0:T])

            wait_taken(act, "table")
            with act.Fori(0, E) as e:
                blocks = act.value_load(table[0:1, bass.ds(e, 1)], min_val=1, max_val=MAXB)
                first = act.value_load(table[0:1, bass.ds(e + E, 1)], min_val=0, max_val=MAXB * E)
                with act.Fori(0, blocks) as c:
                    w1 = act.snap(first + c + 1)
                    act.wait_ge(sem["xb_psum"], w1)
                    fn(xbT, bank_a[:, :].rearrange("p (k r) -> p k r", r=ROWS), ACT.Copy).then_inc(sem["xb_ready"], 1)
                    act.wait_ge(sem["g_clamped"], w1)
                    fn(sg_t, g_t, ACT.Sigmoid, scale=ALPHA).then_inc(sem["sig_ready"], 1)
                    act.wait_ge(sem["comb_psum"], w1)
                    fn(combT, bank_d[:, 0:T], ACT.Copy).then_inc(sem["comb_ready"], 1)
                    act.wait_ge(sem["actT_psum"], w1)
                    fn(actT.rearrange("p (h i) r -> p i h r", h=2), bank_a[:, :].rearrange("p (i h r) -> p i h r", h=2, r=ROWS),
                       ACT.Copy).then_inc(sem["actT_ready"], 1)
                    act.wait_ge(sem["chunk_used"], act.snap(CHUNKS * w1))
                    fn(yb, bank_d[:, :], ACT.Copy).then_inc(sem["yb_ready"], 1)
            for t in range(NT):
                for h in range(2):
                    n = 2 * t + h
                    act.wait_ge(sem["scattered"], t + 1)
                    fn(squares[:, 0:512], bank_y[t][h][:, :], ACT.Square,
                       accum_out=ssq[:, 4 + n:5 + n]).then_inc(sem["out_squared"], 1)
                    act.wait_ge(sem["out_squared"], n + 1)
        @block.vector
        def _(dve):
            v = nc.vector
            steps = [0]

            def link(ins):
                steps[0] += 1
                ins.then_inc(sem["dve_step"], 1)
                dve.wait_ge(sem["dve_step"], steps[0])

            def tiles(job, n):
                return bank_of(job)[:, :].rearrange("p (k t) -> p k t", t=n)

            def inv_rms(dst, src, n):
                w = src.shape[1]
                a, t = newton[:, 0, 0:w], newton[:, 1, 0:w]
                link(v.tensor_scalar(src, src, 1.0 / n, EPS, ALU.mult, ALU.add))
                v.tensor_scalar(a, src, -0.5, None, ALU.mult)
                link(v.tensor_scalar(dst.bitcast(I32), src.bitcast(I32), 1, None, ALU.arith_shift_right))
                link(v.tensor_scalar(dst.bitcast(I32), dst.bitcast(I32), -1.0, float(0x5F3759DF), ALU.mult, ALU.add))
                for _ in range(3):
                    if w == 1:
                        link(v.scalar_tensor_tensor(t, dst, dst, a, ALU.mult, ALU.mult))
                    else:
                        link(v.tensor_tensor(t, dst, dst, ALU.mult))
                        link(v.tensor_tensor(t, t, a, ALU.mult))
                    link(v.scalar_tensor_tensor(dst, t, 1.5, dst, ALU.add, ALU.mult))

            def norm_diag(t, i, squared, diag, signal):
                dve.wait_ge(squared, t + 1)
                inv_rms(rstd[:, i + t:i + t + 1], ssq[:, i + t:i + t + 1], D)
                v.tensor_scalar(diag[:, t, :], ident[:, :], rstd[:, i + t:i + t + 1], None, ALU.mult).then_inc(signal, 1)

            def weigh_tile(prefix, t, dst, w):
                for h in range(2):
                    job = f"{prefix}{t}{h}"
                    wait_full(dve, job)
                    taken(v.tensor_tensor(dst[:, 4 * h:4 * h + 4, t * P:(t + 1) * P], tiles(job, P),
                                          w[:, 4 * h:4 * h + 4].unsqueeze(2).broadcast_to([P, 4, P]), ALU.mult), job)

            def weigh(prefix, dst, w):
                for t in range(NT):
                    weigh_tile(prefix, t, dst, w)

            dve.wait_ge(sem["consts_ready"], 1)
            for t in range(NT):
                norm_diag(t, 0, sem["x_squared"], x_diag, sem["x_diag"])
            dve.wait_ge(sem["w_mix_in"], 16)
            weigh("xT", hT, w_mix)
            dve.wait_ge(sem["lb_in"], 16)
            v.tensor_tensor(lb2[:, 0, :], lb2[:, 0, :], lb2[:, 1, :], ALU.subtract).then_inc(sem["lb_diff"], 1)
            for t in range(NT):
                norm_diag(t, 2, sem["mem_squared"], mem_diag, sem["mem_diag"])
            dve.wait_ge(sem["lb_sigmoid"], 1)
            link(v.tensor_scalar(lb2[:, 1, :], lb2[:, 0, :], -1.0, 1.0, ALU.mult, ALU.add))
            for t in range(NT):
                wait_taken(dve, f"hf{t}")
                link(v.tensor_tensor(f_tok[:, t, :], lb2[:, 1, :], sig_f[:, t, :], ALU.mult))
                v.tensor_tensor(f_tok[:, t, :], f_tok[:, t, :], lb2[:, 0, :], ALU.add).then_inc(sem["f_ready"], 1)
            dve.wait_ge(sem["gk_bias_in"], 16)
            wait_full(dve, "z")
            ins = v.tensor_tensor(zb, tiles("z", 256), gk_bias.unsqueeze(1).broadcast_to([P, NT, 256]), ALU.add)
            taken(ins, "z")
            wait_taken(dve, "z")
            v.scalar_tensor_tensor(ez, zb, -1.0, zb, ALU.mult, ALU.min).then_inc(sem["z_abs"], 1)
            dve.wait_ge(sem["vec_in"], 80)
            weigh("mT", memT, w_mem)
            dve.wait_ge(sem["z_ln"], 1)
            v.scalar_tensor_tensor(g_tok[:, :, 512:768], zb, 0.0, l_z, ALU.min, ALU.subtract).then_inc(sem["g_ready"], 1)
            for i in range(2):
                dve.wait_ge(sem["hq_sigmoid"], i + 1)
                taken(v.tensor_tensor(qT[:, 2 * i:2 * i + 2, :], tiles(f"hq{i}", T),
                                      tmp[:, i, :].rearrange("p (k t) -> p k t", t=T), ALU.mult), f"hq{i}")
            for i in range(2):
                wait_full(dve, f"fT{i}")
                taken(v.tensor_scalar(kT[:, 2 * i:2 * i + 2, :], tiles(f"fT{i}", T), -1.0, 1.0, ALU.mult, ALU.add), f"fT{i}")

            def halves(m, s):
                mm = m.rearrange("p k (b a r) -> p (k b) a r", a=2, r=s)
                return mm[:, :, 0, :], mm[:, :, 1, :]

            def by_chunk(m):
                return m.rearrange("p k (c r) -> p k c r", r=CHUNK)

            def differences(n):
                s = LEVELS[n]
                Rn = R[:, n % 2]
                if n >= 2:
                    for job in level_jobs(LEVELS[n - 2]):
                        wait_full(dve, job)
                if s < CHUNK:
                    b1, b2 = halves(bT, s)
                    r1, r2 = halves(Rn, s)
                    last = b1[:, :, s - 1:s].broadcast_to(list(b1.shape))
                    v.tensor_tensor(r1, last, b1, ALU.subtract)
                    v.tensor_tensor(r2, b2, last, ALU.subtract).then_inc(sem["r_diff"], 1)
                    return
                b, r = by_chunk(bT), by_chunk(Rn)
                ends = b[:, :, :, CHUNK - 1:CHUNK]

                def end_of(c):
                    return ends[:, :, c, :].broadcast_to([P, QT, CHUNK])

                if s == CHUNK:
                    for c in (0, 2):
                        v.tensor_tensor(r[:, :, c, :], end_of(c), b[:, :, c, :], ALU.subtract)
                        ins = v.tensor_copy(r[:, :, c + 1, :], b[:, :, c + 1, :])
                else:
                    v.tensor_tensor(r[:, :, 1, :], end_of(1), b[:, :, 1, :], ALU.subtract)
                    v.tensor_copy(r[:, :, 2, :], b[:, :, 2, :])
                    v.tensor_tensor(r[:, :, 3, :], b[:, :, 3, :], end_of(2), ALU.add)
                    link(v.tensor_tensor(r[:, :, 0, :], end_of(0), b[:, :, 0, :], ALU.subtract))
                    ins = v.tensor_tensor(r[:, :, 0, :], r[:, :, 0, :], end_of(1), ALU.add)
                ins.then_inc(sem["r_diff"], 1)

            def decayed(n):
                s = LEVELS[n]
                r1, r2 = halves(R[:, n % 2], s)
                k1, _ = halves(kT, s)
                _, q2 = halves(qT, s)
                dve.wait_ge(sem["r_exp"], n + 1)
                v.tensor_tensor(r1, r1, k1, ALU.mult)
                v.tensor_tensor(r2, r2, q2, ALU.mult).then_inc(sem["r_ready"], 1)

            def take_scores(n):
                s = LEVELS[n]
                mask = masks[:, n, :].bitcast(I32)
                for t in range(NT):
                    job = f"lv{s}_h{t}"
                    wait_full(dve, job)
                    taken(v.copy_predicated(S[:, 0:HEADS, t, :], mask.unsqueeze(1).broadcast_to([P, HEADS, P]), tiles(job, P)), job)
                for half in range(2):
                    job = f"lv{s}_g{half}"
                    wait_full(dve, job)
                    src = bank_of(job)[:, :].rearrange("p (h t i) -> p h t i", h=2, t=NT)
                    taken(v.copy_predicated(S_gla(half)[:, :, 0:NT, :],
                                            mask.unsqueeze(1).unsqueeze(1).broadcast_to([P, 2, NT, P]), src), job)

            def gate(name, g):
                for t in range(NT):
                    job = f"{name}{t}"
                    dve.wait_ge(sem["gate_sigmoid"], 2 * g + t + 1)
                    dst = gates[:, t, g * 512:(g + 1) * 512]
                    taken(v.tensor_tensor(dst, bank_of(job)[:, :], tmp[:, t, :], ALU.mult), job)
                    wait_taken(dve, job)
                    d4 = dst.rearrange("p (h n) -> p h n", n=VD)
                    v.tensor_tensor(d4, d4, onorm[:, g * VD:(g + 1) * VD].unsqueeze(1).broadcast_to([P, HEADS, VD]),
                                    ALU.mult).then_inc(sem["gate_ready"], 1)

            for job in ("b0", "b1", "b2"):
                wait_taken(dve, job)
            differences(0)
            differences(1)
            for job in ("gq", "gk", "hq0", "hq1", "fT0", "fT1"):
                wait_taken(dve, job)
            decayed(0)
            decayed(1)
            dve.wait_ge(sem["s_zeroed"], 1)
            dve.wait_ge(sem["masks_ready"], len(LEVELS) - 1)
            for n in range(7):
                if n in (2, 3):
                    gate(("hg", "gg")[n - 2], n - 2)
                take_scores(n)
                if n + 2 < 8:
                    differences(n + 2)
                    decayed(n + 2)
            v.tensor_tensor(R[:, 0], qT, kT, ALU.mult).then_inc(sem["r_ready"], 1)

            wait_taken(dve, "diag")
            for t in range(NT):
                for g, group in enumerate("hg"):
                    job = f"o{t}{group}"
                    wait_full(dve, job)
                    for h in range(HEADS):
                        hh = g * HEADS + h
                        ins = v.scalar_tensor_tensor(o_tok[:, t, hh * VD:(hh + 1) * VD], v_tok[:, t, hh * VD:(hh + 1) * VD],
                                                     dots[:, t, hh:hh + 1], bank_of(job)[:, h * VD:(h + 1) * VD], ALU.mult, ALU.add)
                    taken(ins, job)
                    wait_taken(dve, job)
                ot = o_tok[:, t, :]
                o8 = ot.rearrange("p (h n) -> p h n", n=VD)
                link(v.tensor_tensor(xn[:, t, :], ot, ot, ALU.mult))
                link(v.tensor_reduce(hsq[:, t, :], xn[:, t, :].rearrange("p (h n) -> p h n", n=VD), AX.X, ALU.add))
                inv_rms(hrms[:, t, :], hsq[:, t, :], VD)
                link(v.tensor_tensor(o8, o8, hrms[:, t, :].unsqueeze(2).broadcast_to([P, 2 * HEADS, VD]), ALU.mult))
                v.tensor_tensor(ot, ot, gates[:, t, :], ALU.mult).then_inc(sem["y_ready"], 1)

            def add_rows(prefix, t):
                for h in range(2):
                    job = f"{prefix}{h}{t}"
                    wait_full(dve, job)
                    dst = x_res[:, t, h * 512:(h + 1) * 512]
                    taken(v.tensor_tensor(dst, dst, bank_of(job)[:, :], ALU.add), job)

            for t in range(NT):
                add_rows("out", t)
                norm_diag(t, 4, sem["x1_squared"], x1_diag, sem["x1_diag"])
            weigh("aT", aT, w_xa)
            for h in range(2):
                for t in range(NT):
                    wait_full(dve, f"sc{t}{h}")
                    v.tensor_reduce(nmax[:, t, 2 * h:2 * h + 2], tiles(f"sc{t}{h}", T), AX.X, ALU.max,
                                    negate=True).then_inc(sem["neg_max"], 1)
            for h in range(2):
                for t in range(NT):
                    wait_taken(dve, f"sc{t}{h}")
                    r = psums[:, t, 2 * h:2 * h + 2]
                    link(v.reciprocal(r, r))
                    p2 = probs[:, t, 2 * h:2 * h + 2, :]
                    v.tensor_tensor(p2, p2, r.unsqueeze(2).broadcast_to([P, 2, T]), ALU.mult).then_inc(sem["p_ready"], 1)
            def experts_input(t):
                v.scalar_tensor_tensor(h2[:, t, :], x_res[:, t, :], rstd[:, 6 + t:7 + t], norm_row, ALU.mult,
                                       ALU.mult).then_inc(sem["h2_ready"], 1)

            def choose(t):
                wait_full(dve, f"router{t}")
                taken(v.tensor_tensor(logits[:, t, :], bank_of(f"router{t}")[:, 0:E], b_router, ALU.add), f"router{t}")
                wait_taken(dve, f"router{t}")
                link(v.max(top8[:, t, :], logits[:, t, :]))
                v.tensor_scalar(ngmax[:, t:t + 1], top8[:, t, 0:1], -1.0, None, ALU.mult).then_inc(sem["gate_max"], 1)
                link(v.max_index(idx8[:, t * 8:(t + 1) * 8], top8[:, t, :], logits[:, t, :]))
                link(v.tensor_copy(idxf[:, t, :], idx8[:, t * 8:(t + 1) * 8]))
                for r in range(TOPK):
                    if r == 0:
                        link(v.tensor_scalar(chosen[:, t, :], iota[:, 0:E], idxf[:, t, r:r + 1], None, ALU.is_equal))
                    else:
                        ins = v.scalar_tensor_tensor(chosen[:, t, :], iota[:, 0:E], idxf[:, t, r:r + 1], chosen[:, t, :],
                                                     ALU.is_equal, ALU.add)
                        if r < TOPK - 1:
                            link(ins)
                ins.then_inc(sem["chosen_ready"], 1)

            for i in (1, 2):
                g = slice(BIAS_PARTS[i], P)
                dve.wait_ge(sem["gu_part_ready"], i)
                v.tensor_tensor(b_gu_raw[g, :], b_gu_raw[g, :], b_gu[g, :], ALU.subtract).then_inc(sem["gu_rest_ready"], 1)
            add_rows("xo", 0)
            norm_diag(0, 6, sem["x2_squared"], x2_diag, sem["x2_diag"])
            dve.wait_ge(sem["moe_row_in"], 16)
            experts_input(0)
            add_rows("xo", 1)
            weigh_tile("eT", 0, h2T, w_moe)
            norm_diag(1, 6, sem["x2_squared"], x2_diag, sem["x2_diag"])
            experts_input(1)
            weigh_tile("eT", 1, h2T, w_moe)
            v.memset(selg[:, :, :], 0.0)
            dve.wait_ge(sem["router_in"], 32)
            for t in range(NT):
                choose(t)
            dve.wait_ge(sem["chosen_ready"], NT)
            dve.wait_ge(sem["gate_exps"], NT)
            link(v.tensor_tensor(gate_tok, gate_ex, chosen, ALU.mult))
            link(v.tensor_reduce(gsum, gate_tok, AX.X, ALU.add))
            link(v.reciprocal(gsum, gsum))
            link(v.tensor_tensor(gate_tok, gate_tok, gsum.unsqueeze(2).broadcast_to([P, NT, E]), ALU.mult))
            v.tensor_copy(selg[:, :, :].rearrange("p t (h r) -> p t h r", h=2)[:, :, :, 0:E],
                          gate_tok.unsqueeze(2).broadcast_to([P, NT, 2, E])).then_inc(sem["gates_ready"], 1)
            wait_full(dve, "count")
            count = bank_of("count")[0:E, 0:1]
            link(v.tensor_scalar(nb_col, count, float(ROWS), 1.0, ALU.is_gt, ALU.add))
            for m in range(2, MAXB):
                ins = v.scalar_tensor_tensor(nb_col, count, float(m * ROWS), nb_col, ALU.is_gt, ALU.add)
                if m < MAXB - 1:
                    link(ins)
            taken(ins, "count")
            wait_full(dve, "rank")
            ins = v.scalar_tensor_tensor(rank_m, bank_of("rank")[:, 0:NT * E].rearrange("p (t e) -> p t e", e=E), 1.0, chosen,
                                         ALU.add, ALU.mult)
            taken(ins, "rank")
            wait_taken(dve, "rank")
            link(v.tensor_scalar(rank_m, rank_m, -1.0, None, ALU.add))
            wait_full(dve, "table")
            rows = bank_of("table")[0:1, :]
            v.tensor_copy(table_f[0:1, 0:2 * E], rows[0:1, 0:2 * E])
            link(v.tensor_scalar(table_f[0:1, 2 * E:3 * E], rows[0:1, E:2 * E], float(CHUNKS), -float(CHUNKS), ALU.mult, ALU.add))
            v.tensor_copy(table[0:1, 0:2 * E], rows[0:1, 0:2 * E])
            v.tensor_scalar(table[0:1, 2 * E:3 * E], table_f[0:1, 2 * E:3 * E], 0.0, None, ALU.max)
            taken(v.tensor_tensor(table[0:1, 3 * E:3 * E + 1], table_f[0:1, E - 1:E], table_f[0:1, 2 * E - 1:2 * E], ALU.add), "table")
            wait_taken(dve, "table")

            with dve.Fori(0, E) as e:
                blocks = dve.value_load(table[0:1, bass.ds(e, 1)], min_val=1, max_val=MAXB)
                with dve.Fori(0, blocks) as c:
                    rows = iota[:, bass.ds(c * ROWS, ROWS)]
                    v.tensor_copy(one_hot, ident3[:, bass.ds(e, 1)].broadcast_to([P, ROWS]))
                    for t in range(NT):
                        ins = v.tensor_scalar(sel[:, t, :], rows, rank_m[:, t, bass.ds(e, 1)], None, ALU.is_equal)
                    ins.then_inc(sem["sel_ready"], 1)
                    first = dve.value_load(table[0:1, bass.ds(e + E, 1)], min_val=0, max_val=MAXB * E)
                    w1 = dve.snap(first + c + 1)
                    dve.wait_ge(sem["gate_done"], w1)
                    v.tensor_scalar(g_t, bank_g[:, :], LIMIT, None, ALU.min).then_inc(sem["g_clamped"], 1)
                    dve.wait_ge(sem["chunk_used"], dve.snap(CHUNKS * w1 - (CHUNKS - GU_CHUNKS)))
                    v.tensor_scalar(u_t, bank_u[:, :], LIMIT, -LIMIT, ALU.min, ALU.max).then_inc(sem["u_clamped"], 1)
                    for t in range(NT):
                        for half in range(2):
                            ins = v.tensor_scalar(selg[:, t, half * ROWS:(half + 1) * ROWS], rows, rank_m[:, t, bass.ds(e, 1)],
                                                  gate_tok[:, t, bass.ds(e, 1)], ALU.is_equal, ALU.mult)
                    ins.then_inc(sem["selg_ready"], 1)
                    dve.wait_ge(sem["u_clamped"], w1)
                    v.scalar_tensor_tensor(u_t, u_t, 1.0, g_t, ALU.add, ALU.mult).then_inc(sem["up_gated"], 1)
                    dve.wait_ge(sem["up_gated"], w1)
                    dve.wait_ge(sem["sig_ready"], w1)
                    v.tensor_tensor(act_t, u_t, sg_t, ALU.mult).then_inc(sem["act_ready"], 1)
            dve.wait_ge(sem["final_row_in"], 16)
            for t in range(NT):
                dve.wait_ge(sem["out_squared"], 2 * t + 2)
                link(v.tensor_tensor(ssq[:, t:t + 1], ssq[:, 4 + 2 * t:5 + 2 * t], ssq[:, 5 + 2 * t:6 + 2 * t], ALU.add))
                inv_rms(rstd[:, t:t + 1], ssq[:, t:t + 1], D)
                for h in range(2):
                    c = slice(h * 512, (h + 1) * 512)
                    v.scalar_tensor_tensor(xn[:, t, c], bank_y[t][h][:, :], rstd[:, t:t + 1], norm_row[:, c], ALU.mult,
                                           ALU.mult).then_inc(sem["out_ready"], 1)


_INS = ["x", "mem", "norm_mix_w", "w_in", "hg_lb_logits", "hg_onorm_w", "gla_w_gk2", "gla_b_gk", "gla_onorm_w", "w_out",
        "norm_xa_w", "norm_mem_w", "w_xq", "w_xkv", "w_xo", "norm_moe_w", "w_router", "b_router", "w_gate_up",
        "b_gate_up", "w_down", "b_down", "norm_final_w"]


def kernel(**inputs):
    import concourse.bacc as bacc
    from concourse.bass_utils import run_bass_kernel_spmd

    nc = bacc.Bacc("TRN2", target_bir_lowering=False, num_devices=1)
    arrays, aps = {}, {}
    for name in _INS:
        a = np.ascontiguousarray(inputs[name])
        arrays[f"in_{name}"] = a
        aps[name] = nc.dram_tensor(f"in_{name}", a.shape, mybir.dt.from_np(a.dtype), kind="ExternalInput").ap()
    out = nc.dram_tensor("out_0", (1, T, D), F32, kind="ExternalOutput").ap()
    build(nc, aps, out)
    result = run_bass_kernel_spmd(nc, [arrays], core_ids=[0])
    return result.results[0]["out_0"]
```
